# Optimizing a Trainium2 kernel written in Bass

```python
import jax, jax.numpy as jnp
from jax import lax
import numpy as np

D_MODEL = 2048
BATCH = 1
SEQ = 128
DEPTH = 1
DEC_BATCH = 1
DEC_SEQ = 256
PAST_LEN = 128

GRID_W = 64
HEAD_DIM = 128
D_MIX = D_MODEL
D_ATTN = D_MIX // 2
D_CONV = D_MIX - D_ATTN
N_HEADS = D_ATTN // HEAD_DIM
N_KV_HEADS = 2
GQA_GROUP = N_HEADS // N_KV_HEADS
D_KV = N_KV_HEADS * HEAD_DIM
CONV_WIDTH = 3
N_EXPERTS = 16
EC_CAPACITY_FACTOR = 2
D_FF_EXPERT = D_MODEL // 2
Q_BLOCK = 128
ROPE_THETA = 10000.0
RMS_EPS = 1e-6
D_IN_PROJ = D_ATTN + 2 * D_KV + 3 * D_CONV
N_MOD = 6

kernel_name = "hybrid_attn_shortconv_ec_moe_dit_step"

def rms_norm(x, g):
    xf = x.astype(jnp.float32)
    y = xf * lax.rsqrt(jnp.mean(xf * xf, axis=-1, keepdims=True) + RMS_EPS)
    return (y * g.astype(jnp.float32)).astype(x.dtype)

def ada_modulation(cond, w_ada, b_ada):
    m = jax.nn.silu(cond) @ w_ada + b_ada
    return [p[:, None, :] for p in jnp.split(m, N_MOD, axis=-1)]

def axial_rope(x, rows):
    t = jnp.arange(rows * GRID_W)
    row = (t // GRID_W).astype(jnp.float32)
    col = (t % GRID_W).astype(jnp.float32)
    half = HEAD_DIM // 2
    inv_freq = ROPE_THETA ** (-jnp.arange(0, half, 2, dtype=jnp.float32) / half)

    def rotate(xa, pos):
        ang = pos[:, None] * inv_freq[None, :]
        cos = jnp.cos(ang)[None, :, None, :]
        sin = jnp.sin(ang)[None, :, None, :]
        x1, x2 = jnp.split(xa, 2, axis=-1)
        return jnp.concatenate([x1 * cos - x2 * sin, x1 * sin + x2 * cos], axis=-1)

    xf = x.astype(jnp.float32)
    out = jnp.concatenate([rotate(xf[..., :half], row), rotate(xf[..., half:], col)], axis=-1)
    return out.astype(x.dtype)

def block_attention(q, k, v):
    B, T = q.shape[0], q.shape[1]
    nb = T // Q_BLOCK
    qb = q.reshape(B, nb, Q_BLOCK, N_KV_HEADS, GQA_GROUP, HEAD_DIM).transpose(1, 0, 2, 3, 4, 5)
    scale = HEAD_DIM ** -0.5

    def one_block(qblk):
        s = jnp.einsum('bqkgd,bskd->bkgqs', qblk, k).astype(jnp.float32) * scale
        p = jax.nn.softmax(s, axis=-1).astype(v.dtype)
        return jnp.einsum('bkgqs,bskd->bqkgd', p, v)

    o = lax.map(one_block, qb)
    return o.transpose(1, 0, 2, 3, 4, 5).reshape(B, T, D_ATTN)

def short_conv(u, w):
    up = jnp.pad(u, ((0, 0), (1, 1), (0, 0)))
    return up[:, :-2] * w[0] + up[:, 1:-1] * w[1] + up[:, 2:] * w[2]

def ec_moe(h, w_router, w_gate, w_up, w_down):
    B, T, D = h.shape
    cap = EC_CAPACITY_FACTOR * T // N_EXPERTS
    logits = jnp.einsum('btd,de->bte', h, w_router).astype(jnp.float32)
    aff = jax.nn.softmax(logits, axis=-1)
    gate, idx = lax.top_k(jnp.swapaxes(aff, 1, 2), cap)
    xs = jax.vmap(lambda hb, ib: hb[ib])(h, idx)
    a = jnp.einsum('becd,edf->becf', xs, w_gate)
    u = jnp.einsum('becd,edf->becf', xs, w_up)
    y = jnp.einsum('becf,efd->becd', jax.nn.silu(a) * u, w_down)
    y = y * gate[..., None].astype(y.dtype)
    return jax.vmap(lambda ib, yb: jnp.zeros((T, D), yb.dtype).at[ib.reshape(-1)].add(yb.reshape(-1, D)))(idx, y)

def trunk_layer(x, cond, ctx_kv, rows, w_ada, b_ada, g_norm1, w_in, g_q, g_k, conv_w,
                g_attn_out, g_conv_out, w_out, g_norm2, w_router, w_gate, w_up, w_down):
    B, T, _ = x.shape
    sh1, sc1, g1, sh2, sc2, g2 = ada_modulation(cond, w_ada, b_ada)
    h = rms_norm(x, g_norm1) * (1 + sc1) + sh1
    proj = h @ w_in
    q, k, v, bg, cg, u = jnp.split(
        proj, [D_ATTN, D_ATTN + D_KV, D_ATTN + 2 * D_KV, D_ATTN + 2 * D_KV + D_CONV,
               D_ATTN + 2 * D_KV + 2 * D_CONV], axis=-1)
    q = rms_norm(q.reshape(B, T, N_HEADS, HEAD_DIM), g_q)
    k = rms_norm(k.reshape(B, T, N_KV_HEADS, HEAD_DIM), g_k)
    v = v.reshape(B, T, N_KV_HEADS, HEAD_DIM)
    if ctx_kv is None:
        attn = block_attention(q, k, v)
    else:
        q = axial_rope(q, rows)
        k = axial_rope(k, rows)
        k_ctx, v_ctx = ctx_kv
        attn = block_attention(q, jnp.concatenate([k_ctx, k], axis=1),
                               jnp.concatenate([v_ctx, v], axis=1))
    conv_out = bg * short_conv(cg * u, conv_w)
    mixed = jnp.concatenate([rms_norm(attn, g_attn_out), rms_norm(conv_out, g_conv_out)], axis=-1)
    x = x + g1 * (mixed @ w_out)
    h2 = rms_norm(x, g_norm2) * (1 + sc2) + sh2
    x = x + g2 * ec_moe(h2, w_router, w_gate, w_up, w_down)
    return x, k, v

def setup_inputs(seed: int = 0) -> dict:
    key = jax.random.key(seed)
    ks = jax.random.split(key, 24)
    f32 = jnp.float32
    nrm = lambda k, shape, s: jax.random.normal(k, shape, f32) * s
    d_in_s = D_MODEL ** -0.5
    return {
        "x_prompt": nrm(ks[0], (BATCH, SEQ, D_MODEL), 1.0),
        "x_sample": nrm(ks[1], (DEC_BATCH, DEC_SEQ, D_MODEL), 1.0),
        "cache_k": nrm(ks[2], (DEC_BATCH, DEPTH, PAST_LEN, N_KV_HEADS, HEAD_DIM), 1.0),
        "cache_v": nrm(ks[3], (DEC_BATCH, DEPTH, PAST_LEN, N_KV_HEADS, HEAD_DIM), 1.0),
        "c": nrm(ks[4], (DEC_BATCH, D_MODEL), 1.0),
        "c_ctx": nrm(ks[5], (D_MODEL,), 1.0),
        "w_ada": nrm(ks[6], (DEPTH, D_MODEL, N_MOD * D_MODEL), 0.5 * d_in_s),
        "b_ada": nrm(ks[7], (DEPTH, N_MOD * D_MODEL), 0.02),
        "g_norm1": 1.0 + nrm(ks[8], (DEPTH, D_MODEL), 0.02),
        "w_in": nrm(ks[9], (DEPTH, D_MODEL, D_IN_PROJ), d_in_s),
        "g_q": 1.0 + nrm(ks[10], (DEPTH, HEAD_DIM), 0.02),
        "g_k": 1.0 + nrm(ks[11], (DEPTH, HEAD_DIM), 0.02),
        "conv_w": nrm(ks[12], (DEPTH, CONV_WIDTH, D_CONV), CONV_WIDTH ** -0.5),
        "g_attn_out": 1.0 + nrm(ks[13], (DEPTH, D_ATTN), 0.02),
        "g_conv_out": 1.0 + nrm(ks[14], (DEPTH, D_CONV), 0.02),
        "w_out": nrm(ks[15], (DEPTH, D_MIX, D_MODEL), D_MIX ** -0.5),
        "g_norm2": 1.0 + nrm(ks[16], (DEPTH, D_MODEL), 0.02),
        "w_router": nrm(ks[17], (DEPTH, D_MODEL, N_EXPERTS), d_in_s),
        "w_gate": nrm(ks[18], (DEPTH, N_EXPERTS, D_MODEL, D_FF_EXPERT), d_in_s),
        "w_up": nrm(ks[19], (DEPTH, N_EXPERTS, D_MODEL, D_FF_EXPERT), d_in_s),
        "w_down": nrm(ks[20], (DEPTH, N_EXPERTS, D_FF_EXPERT, D_MODEL), D_FF_EXPERT ** -0.5),
    }

def reference(x_prompt, x_sample, cache_k, cache_v, c, c_ctx, w_ada, b_ada, g_norm1, w_in,
              g_q, g_k, conv_w, g_attn_out, g_conv_out, w_out, g_norm2, w_router, w_gate,
              w_up, w_down):
    rows = x_sample.shape[1] // GRID_W
    y_prompt = x_prompt
    y_sample = x_sample
    new_k = []
    new_v = []
    for l in range(DEPTH):
        params = (w_ada[l], b_ada[l], g_norm1[l], w_in[l], g_q[l], g_k[l], conv_w[l],
                  g_attn_out[l], g_conv_out[l], w_out[l], g_norm2[l], w_router[l],
                  w_gate[l], w_up[l], w_down[l])
        y_prompt, k_ctx, v_ctx = trunk_layer(y_prompt, c_ctx[None, :], None, 0, *params)
        new_k.append(k_ctx)
        new_v.append(v_ctx)
        y_sample, _, _ = trunk_layer(y_sample, c, (cache_k[:, l], cache_v[:, l]), rows, *params)
    state_k = jnp.stack(new_k, axis=1)
    state_v = jnp.stack(new_v, axis=1)
    return (y_prompt, y_sample, state_k, state_v)


_drawn_inputs = setup_inputs


def setup_inputs(seed=0):
    import zlib

    import numpy as np

    out = dict(_drawn_inputs(seed))
    spreads = {}
    factors = {'g_norm1': 2.997, 'g_q': 8.0, 'g_attn_out': 8.0, 'g_conv_out': 8.0, 'g_norm2': 8.0}
    for name, (base, spread) in spreads.items():
        noise = np.random.default_rng([zlib.crc32(name.encode()), seed]).standard_normal(out[name].shape)
        drawn = base * np.exp(spread * noise) if base else spread * noise
        out[name] = __import__('jax').numpy.asarray(drawn.astype(out[name].dtype))
    for name, factor in factors.items():
        out[name] = (out[name] * factor).astype(out[name].dtype)
    return out
```

```python
from contextlib import ExitStack

import numpy as np

import concourse.bass as bass
from concourse import mybir

F32 = mybir.dt.float32
ALU = mybir.AluOpType
ACT = mybir.ActivationFunctionType
AX_X = mybir.AxisListType.X

P = 128
D = 2048
KC = D // P
T_CTX, T_LAT = 128, 256
T = T_CTX + T_LAT
NT = T // P
HD = 128
NH, NKV = 8, 2
GROUP = NH // NKV
D_ATTN = NH * HD
D_CONV = D - D_ATTN
AC = D_ATTN // P
CCH = D_CONV // P
D_KV = NKV * HD
D_IN = D_ATTN + 2 * D_KV + 3 * D_CONV
N_MOD = 6
NE = 16
FF = D // 2
FC = FF // P
CAP_CTX, CAP_LAT = 2 * T_CTX // NE, 2 * T_LAT // NE
CAP = CAP_CTX + CAP_LAT
PAIRS = NE // 2
ES = 64
PW = 2 * ES
GRID_W = 64
EPS = 1e-6
SCALE = HD ** -0.5
SLOT = 4096
BLK = 512
BANK = 512

COLS = [(0, T_CTX), (T_CTX, T)]

C_ID, C_ROPE, C_IOTA = 0, P, P + 256
C_ALL = C_IOTA + ES

V_C, V_CTX, V_G1, V_G2, V_GA, V_GC, V_TAP = 0, 16, 32, 48, 64, 72, 80
V_ALL = V_TAP + 3 * CCH

MATS = [("g", 0), ("u", 0), ("g", 1), ("d", 0), ("u", 1), ("d", 1)]
PER_PAIR = 4 * len(MATS)
RING = 8
FREE = 1
ORDER = [4, 5, 6, 7, 2, 3, 0, 1]


def build(nc, x_prompt, x_sample, cache_k, cache_v, c, c_ctx, w_ada, b_ada, g_norm1, w_in, g_q, g_k, conv_w,
          g_attn_out, g_conv_out, w_out, g_norm2, w_router, w_gate, w_up, w_down, consts,
          y_prompt, y_sample, state_k, state_v):
    with ExitStack() as ctx:
        def sb(name, shape):
            return ctx.enter_context(nc.sbuf_tensor(name, shape, F32))

        def sem(name):
            return ctx.enter_context(nc.semaphore(name))

        ring = sb("ring", [P, RING, SLOT])
        res = sb("res", [P, KC * T])
        hid = sb("hid", [P, KC * T])
        mix = sb("mix", [P, KC * T])

        xT = res[:, :].rearrange("p (k t) -> p k t", k=KC)
        hT = hid[:, :].rearrange("p (k t) -> p k t", k=KC)
        mixT = mix[:, :].rearrange("p (k t) -> p k t", k=KC)
        x_rows = mix[:, :].rearrange("p (n d) -> p n d", n=NT)
        h2_rows = x_rows
        y_rows = x_rows
        q_rows = mix[:, 0:NT * D_ATTN].rearrange("p (n d) -> p n d", n=NT)
        tmp_a = mix[:, 3072:3072 + D_ATTN]
        tmp_b = mix[:, 3072 + D_ATTN:3072 + 2 * D_ATTN]
        mod_rows = [mix[:, KC * T - BANK:], mix[:, KC * T - 2 * BANK:KC * T - BANK]]

        front = ring[:, 4:7, :].rearrange("p s n -> p (s n)")
        at = [0]

        def piece(n):
            at[0] += n
            assert at[0] <= 3 * SLOT
            return front[:, at[0] - n:at[0]]

        kv_rows = piece(NT * 2 * D_KV).rearrange("p (n d) -> p n d", n=NT)
        qT = piece(NH * T).rearrange("p (h t) -> p h t", h=NH)
        kT = piece(NKV * 512).rearrange("p (h t) -> p h t", h=NKV)
        kc = piece(D_KV)
        vc = piece(D_KV)
        prob_flat = piece(2 * T)
        prob = prob_flat.rearrange("p (n t) -> p n t", n=2)
        vec_rows, bias_rows = prob_flat[0:V_ALL, 0:P], prob_flat[0:6 * KC, P:2 * P]
        probT = piece(3 * T_LAT).rearrange("p (j t) -> p j t", j=3)
        cu = piece(4 * T).rearrange("p (j t) -> p j t", j=4)
        cv = piece(T)
        sq = [piece(T), piece(T)]
        ssum = [piece(T), piece(T)]
        rstd = [piece(T), piece(T)]
        gqk = piece(2 * HD)
        ada_buf = [ring[:, 7, 0:D], ring[:, 7, D:2 * D]]
        sq2 = [hT[:, KC - 1, :], hT[:, KC - 2, :]]
        ssum2 = hT[:, KC - 3, :]
        rt = ring[:, 1, :]
        rstd2 = rt[:, 0:T]
        affT, work, mask, rank = (rt[0:NE, n * T:(n + 1) * T] for n in (1, 2, 3, 4))
        lg = rt[:, 5 * T:5 * T + NT * NE].rearrange("p (n e) -> p n e", n=NT)
        r_small = rt[:, 5 * T + 64:5 * T + 64 + 16]
        top8 = rt[0:NE, 5 * T + 96:5 * T + 96 + 8]

        ident = sb("ident", [P, P])
        iota = sb("iota", [P, ES])
        early = sb("early", [P, 32 * KC + KC * NE + P + 256])
        cond = early[:, 0:32 * KC].rearrange("p (k n) -> p k n", k=KC)
        wr = early[:, 32 * KC:32 * KC + KC * NE].rearrange("p (k e) -> p k e", k=KC)
        ones = early[:, 32 * KC + KC * NE:32 * KC + KC * NE + P]
        rope = early[:, 32 * KC + KC * NE + P:]
        give = early[:, 0:12 * ES]
        pick = early[:, 12 * ES:18 * ES]
        vecT = sb("vecT", [P, V_ALL])
        biasT = sb("biasT", [P, N_MOD * KC])
        mod3 = sb("mod", [P, N_MOD * KC, 2])
        gain = sb("gain", [P, 2, KC, 2])
        stat = sb("stat", [P, 32])
        slotP = sb("slotP", [P, 6 * PAIRS + 6])
        affP = sb("affP", [P, 6 * PAIRS + 6])

        moe_at = [0]

        def moe_piece(n):
            moe_at[0] += n
            assert moe_at[0] <= KC * T
            return hid[:, moe_at[0] - n:moe_at[0]]

        xs = moe_piece(KC * PW).rearrange("p (k s) -> p k s", k=KC)
        act = moe_piece(BANK)
        actT = moe_piece(BANK)
        y_sb = [moe_piece(2 * BANK), moe_piece(2 * BANK)]
        giveT = [moe_piece(T), moe_piece(T)]

        bank = [ctx.enter_context(nc.psum_tensor(f"bank{i}", [P, BANK], F32)) for i in range(8)]

        small_in, cache_in, wr_in = sem("small_in"), sem("cache_in"), sem("wr_in")
        x_in = [sem(f"x_in{n}") for n in range(NT)]
        w_landed = [sem(f"w_landed{n}") for n in range(4)]
        w_used = sem("w_used")
        ada_landed = [sem("ada_landed0"), sem("ada_landed1")]
        ada_free = sem("ada_free")
        moe_landed = [sem(f"moe_landed{n}") for n in range(RING)]
        moe_used = sem("moe_used")
        set_up, vec_turned, vec_ready, cond_ready = sem("set_up"), sem("vec_turned"), sem("vec_ready"), sem("cond_ready")
        x_turned, x_out_dve, x_out_act = sem("x_turned"), sem("x_out_dve"), sem("x_out_act")
        sq_ready, sq_added, sums_done = sem("sq_ready"), sem("sq_added"), sem("sums_done")
        var_ready, std_ready = sem("var_ready"), sem("std_ready")
        gains_ready, mod_rows_out, mod_turned, mod_read = sem("gains_ready"), sem("mod_rows_out"), sem("mod_turned"), sem("mod_read")
        h_dve, h_act = sem("h_dve"), sem("h_act")
        qkv_acc, qkv_out = sem("qkv_acc"), sem("qkv_out")
        conv_acc, conv_out = sem("conv_acc"), sem("conv_out")
        qk_ready, qk_turned, qkT_ready = sem("qk_ready"), sem("qk_turned"), sem("qkT_ready")
        score_done, max_ready, exp_done, prob_ready = sem("score_done"), sem("max_ready"), sem("exp_done"), sem("prob_ready")
        prob_turned, probT_ready, o_done, o_out = sem("prob_turned"), sem("probT_ready"), sem("o_done"), sem("o_out")
        osq_ready, osq_added = sem("osq_ready"), sem("osq_added")
        csq_ready, csq_added = sem("csq_ready"), sem("csq_added")
        mix_ready = sem("mix_ready")
        out_acc, x1_ready = sem("out_acc"), sem("x1_ready")
        sq2_ready, sq2_added = sem("sq2_ready"), sem("sq2_added")
        h2n_ready, h2_ready = sem("h2n_ready"), sem("h2_ready")
        logits_done, shifted, exp2_done, aff_ready = sem("logits_done"), sem("shifted"), sem("exp2_done"), sem("aff_ready")
        aff_turned, rank_ready, rank_turned, routed = sem("aff_turned"), sem("rank_ready"), sem("rank_turned"), sem("routed")
        rows_turned, rows_out = sem("rows_turned"), sem("rows_out")
        pick_ready, gathered, xs_dve, xs_act = sem("pick_ready"), sem("gathered"), sem("xs_dve"), sem("xs_act")
        give_ready, blank, give_turned, giveT_ready = sem("give_ready"), sem("blank"), sem("give_turned"), sem("giveT_ready")
        sil_ready, act_ready, act_turned, actT_ready = sem("sil_ready"), sem("act_ready"), sem("act_turned"), sem("actT_ready")
        y_out, sent, added = sem("y_out"), sem("sent"), sem("added")
        last_turned, last_dve, last_act = sem("last_turned"), sem("last_dve"), sem("last_act")
        dve_chain, act_chain = sem("dve_chain"), sem("act_chain")
        state_out, y_stored = sem("state_out"), sem("y_stored")

        ada_rows = w_ada[0]
        in_rows = w_in[0].rearrange("(k p) n -> p k n", p=P)
        out_rows = w_out[0].rearrange("(k p) n -> p k n", p=P)
        gate_rows = w_gate.rearrange("a e d f -> (a e d) f")
        up_rows = w_up.rearrange("a e d f -> (a e d) f")
        down_rows = w_down.rearrange("a e f d -> (a e f) d")

        o_b = D_ATTN + 2 * D_KV
        o_c, o_u = o_b + D_CONV, o_b + 2 * D_CONV
        IN_BLOCKS = [0, BLK, 2 * BLK] + [o + h * BLK for h in range(2) for o in (o_u, o_c, o_b)]
        N_ADA1 = KC
        N_IN = 2 * len(IN_BLOCKS)
        N_FRONT = N_ADA1 + N_IN + 2 * (D // BLK)

        class Chain:

            def __init__(self, eng, s):
                self.eng, self.s, self.n, self.base = eng, s, 0, 0

            def link(self, ins):
                self.n += 1
                ins.then_inc(self.s, 1)
                self.eng.wait_ge(self.s, self.base + self.n)

            def enter(self, i, per):
                self.n0, self.per, self.base = self.n, per, i * per

            def leave(self, trips):
                assert self.n - self.n0 == self.per, self.n - self.n0
                self.n, self.base = self.n0 + trips * self.per, 0

        block = ctx.enter_context(nc.Block())

        @block.sync
        def _(sp):
            for n in range(NT):
                src = x_prompt[0] if n == 0 else x_sample[0, (n - 1) * P:n * P, :]
                sp.dma_start(x_rows[:, n, :], src).then_inc(x_in[n], 16)

            for n in range(4):
                sp.dma_start(ring[:, n, :], ada_rows[n * P:(n + 1) * P, 0:SLOT]).then_inc(w_landed[n], 16)
            with sp.Fori(1, N_ADA1 // 4) as i:
                for n in range(4):
                    sp.wait_ge(w_used, 4 * i + (n - 3))
                    sp.dma_start(ring[:, n, :], ada_rows[bass.ds(i * 4 * P + n * P, P), 0:SLOT]).then_inc(w_landed[n], 16)

            def half_free(b, half, more=0):
                if half == 0:
                    sp.wait_ge(w_used, more + (N_ADA1 + b + 1))
                elif b < 3:
                    sp.wait_ge(qkv_acc, NT * (b + 1))
                elif b < 9:
                    sp.wait_ge(conv_acc, 4 * (b - 2))
                else:
                    sp.wait_ge(out_acc, 4 * more + 4 * (b - 8))

            for b, col in enumerate(IN_BLOCKS):
                for half in range(2):
                    n = N_ADA1 + 2 * b + half
                    if b < 2:
                        sp.wait_ge(w_used, n - 3)
                    else:
                        half_free(b - 2, half)
                    sp.dma_start(ring[:, n % 4, :].rearrange("p (k n) -> p k n", n=BLK),
                                 in_rows[:, 8 * half:8 * half + 8, col:col + BLK]).then_inc(w_landed[n % 4], 16)
            for b in range(9, 13):
                for half in range(2):
                    n = N_ADA1 + 2 * b + half
                    half_free(b - 2, half)
                    sp.dma_start(ring[:, n % 4, :].rearrange("p (k n) -> p k n", n=BLK),
                                 out_rows[:, 8 * half:8 * half + 8, (b - 9) * BLK:(b - 8) * BLK]).then_inc(w_landed[n % 4], 16)

            def expert_load(pair, q):
                what, e = MATS[q // 4]
                part, slot = q % 4, ORDER[q % RING]
                if what == "d":
                    rows = down_rows[bass.ds(pair * 2 * FF + e * FF + part * 256, 256), :]
                else:
                    rows = (gate_rows if what == "g" else up_rows)[bass.ds(pair * 2 * D + e * D + part * 512, 512), :]
                sp.dma_start(ring[:, slot, :].rearrange("p (k n) -> p k n", k=2 if what == "d" else 4),
                             rows.rearrange("(k p) n -> p k n", p=P)).then_inc(moe_landed[slot], 16)

            sp.wait_ge(mix_ready, KC)
            sp.wait_ge(state_out, 32)
            for q in range(RING):
                if ORDER[q] == 7:
                    sp.wait_ge(ada_free, 2 + 64)
                if ORDER[q] < 4:
                    half_free(11 if ORDER[q] > 1 else 12, ORDER[q] % 2)
                if ORDER[q] == 1:
                    sp.wait_ge(routed, 1)
                expert_load(0, q)
            with sp.Fori(0, PAIRS - 1) as i:
                for j in range(PER_PAIR):
                    sp.wait_ge(moe_used, PER_PAIR * i + (j + 1))
                    expert_load(i + (j + RING) // PER_PAIR, (j + RING) % PER_PAIR)
            for j in range(PER_PAIR - RING):
                sp.wait_ge(moe_used, PER_PAIR * (PAIRS - 1) + j + 1)
                expert_load(PAIRS - 1, j + RING)

            sp.wait_ge(last_dve, 6)
            sp.wait_ge(last_act, 6)
            sp.dma_start(y_prompt[0], y_rows[:, 0, :]).then_inc(y_stored, 16)
            sp.dma_start(y_sample[0].rearrange("(n p) d -> p n d", p=P), y_rows[:, 1:NT, :]).then_inc(y_stored, 16)
            sp.wait_ge(y_stored, 32)

        @block.gpsimd
        def _(pool):
            nc.gpsimd.memset(ones, 1.0).then_inc(ada_free, 1)
            nc.gpsimd.memset(cond, 0.0).then_inc(ada_free, 1)
            for m in range(2, N_MOD):
                with pool.Fori(0, KC // 2) as i:
                    for j in range(2):
                        pool.wait_ge(ada_free, 2 * i + (KC * (m - 2) + j + 1))
                        pool.dma_start(ada_buf[j], ada_rows[bass.ds(i * 2 * P + j * P, P), m * D:(m + 1) * D])\
                            .then_inc(ada_landed[j], 16)

        @block.tensor
        def _(pe):
            def mm(out, lhsT, rhs, start, stop):
                return nc.tensor.matmul(out, lhsT, rhs, start=start, stop=stop, skip_group_check=True)

            pe.wait_ge(small_in, 16 * 11)
            nc.tensor.transpose(bank[1][:, 0:V_ALL], vec_rows, ident[0:V_ALL, 0:V_ALL])
            nc.tensor.transpose(bank[2][:, 0:N_MOD * KC], bias_rows, ident[0:N_MOD * KC, 0:N_MOD * KC]).then_inc(vec_turned, 1)

            def turn_groups(groups, src, banks, done, free):
                for g in groups:
                    free(g)
                    for j in range(4):
                        last = nc.tensor.transpose(banks[g % len(banks)][:, j * P:(j + 1) * P], src(g, j), ident[:, :])
                    last.then_inc(done, 1)

            def x_free(g):
                if g % 4 == 0:
                    pe.wait_ge(x_in[g // 4], 16)
                if g >= 4:
                    pe.wait_ge(x_out_act if g % 2 else x_out_dve, (g - 4) // 2 + 1)
            turn_groups(range(12), lambda g, j: x_rows[:, g // 4, (g % 4 * 4 + j) * P:(g % 4 * 4 + j + 1) * P],
                        bank[4:8], x_turned, x_free)
            pe.wait_ge(ada_free, 2)
            pe.wait_ge(sq_added, KC)
            mm(bank[3][:, 0:T], ones, ssum[0], True, True).then_inc(sums_done, 1)

            def ada(out, k, weights, first):
                for j in range(4):
                    last = mm(out[32 * j:32 * j + 32, :], cond[:, k, :], weights[:, j * BLK:(j + 1) * BLK], first, k == KC - 1)
                return last

            def turn_mod(out, rows):
                for j in range(4):
                    last = nc.tensor.transpose(out[:, j * P:(j + 1) * P], rows[:, j * P:(j + 1) * P], ident[:, :])
                last.then_inc(mod_turned, 1)

            pe.wait_ge(cond_ready, 1)
            for k in range(N_ADA1):
                pe.wait_ge(w_landed[k % 4], 16 * (k // 4 + 1))
                for m in range(2):
                    last = ada(bank[m], k, ring[:, k % 4, m * D:(m + 1) * D], k == 0)
                last.then_inc(w_used, 1)
            for m in range(2):
                pe.wait_ge(mod_rows_out, m + 1)
                turn_mod(bank[2 + m], mod_rows[m])

            def event(n):
                m, k = 2 + n // (KC + 1), n % (KC + 1)
                if k < KC:
                    t = KC * (m - 2) + k
                    if k == 0 and m > 2:
                        pe.wait_ge(mod_read, m)
                    pe.wait_ge(ada_landed[t % 2], 16 * (t // 2 + 1))
                    ada(bank[0], k, ada_buf[t % 2], k == 0).then_inc(ada_free, 1)
                else:
                    pe.wait_ge(mod_rows_out, m + 1)
                    turn_mod(bank[0], mod_rows[0])

            def w_wait(n):
                pe.wait_ge(w_landed[n % 4], 16 * (n // 4 + 1))

            events = 0
            for b in range(3):
                n = N_ADA1 + 2 * b
                for t in range(NT):
                    g = NT * b + t
                    if g >= 2:
                        pe.wait_ge(qkv_out, g - 1)
                    for k in range(KC):
                        if g == 0:
                            pe.wait_ge(h_act if k % 2 else h_dve, k // 2 + 1)
                        if t == 0 and k % 8 == 0:
                            w_wait(n + k // 8)
                        s = (n + k // 8) % 4
                        last = mm(bank[1 + g % 2][:, :], hT[:, k, t * P:(t + 1) * P],
                                  ring[:, s, (k % 8) * BLK:(k % 8 + 1) * BLK], k == 0, k == KC - 1)
                        if t == NT - 1 and k == 7:
                            last.then_inc(w_used, 1)
                    last.then_inc(qkv_acc, 1)
                    for _ in range(3):
                        event(events)
                        events += 1

            def turn_qk(t):
                pe.wait_ge(qk_ready, t + 1)
                if t:
                    pe.wait_ge(qkT_ready, t)
                for h in range(NH):
                    nc.tensor.transpose(bank[5 + h // 4][:, (h % 4) * P:(h % 4 + 1) * P],
                                        q_rows[:, t, h * HD:(h + 1) * HD], ident[:, :])
                if t == 0:
                    pe.wait_ge(cache_in, 64)
                    for h in range(NKV):
                        nc.tensor.transpose(bank[7][:, (2 + h) * P:(3 + h) * P], kc[:, h * HD:(h + 1) * HD], ident[:, :])
                for h in range(NKV):
                    last = nc.tensor.transpose(bank[7][:, h * P:(h + 1) * P], kv_rows[:, t, h * HD:(h + 1) * HD], ident[:, :])
                last.then_inc(qk_turned, 1)

            def unit(n):
                h = n % NH
                kv = h // GROUP
                v = [kv_rows[:, t, D_KV + kv * HD:D_KV + (kv + 1) * HD] for t in range(NT)]
                if n < NH:
                    return h, [0], kT[:, kv, 0:P], v[0:1]
                return h, [1, 2], kT[:, kv, P:4 * P], [vc[:, kv * HD:(kv + 1) * HD]] + v[1:]

            def scores(n):
                h, tiles, keys, v = unit(n)
                pe.wait_ge(qkT_ready, NT)
                if n:
                    pe.wait_ge(exp_done, n)
                for i, t in enumerate(tiles):
                    last = mm(bank[3 + i][:, 0:len(v) * P], qT[:, h, t * P:(t + 1) * P], keys, True, True)
                last.then_inc(score_done, 1)

            def turn_prob(n):
                h, tiles, keys, v = unit(n)
                pe.wait_ge(prob_ready, n + 1)
                if n:
                    pe.wait_ge(probT_ready, n)
                for j in range(len(v)):
                    for i in range(len(tiles)):
                        last = nc.tensor.transpose(bank[5 + j // 2][:, (2 * (j % 2) + i) * P:(2 * (j % 2) + i + 1) * P],
                                                   prob[:, i, j * P:(j + 1) * P], ident[:, :])
                last.then_inc(prob_turned, 1)

            def values(n):
                h, tiles, keys, v = unit(n)
                w = len(tiles) * P
                pe.wait_ge(probT_ready, n + 1)
                if n:
                    pe.wait_ge(o_out, n)
                for j, vj in enumerate(v):
                    last = mm(bank[7][:, 0:w], vj, probT[:, j, 0:w], j == 0, j == len(v) - 1)
                last.then_inc(o_done, 1)

            for g in range(24):
                b, j = g // 4, g % 4
                n = N_ADA1 + 6 + 2 * b
                if g < 2:
                    pe.wait_ge(qkv_out, 8 + g)
                else:
                    pe.wait_ge(conv_out, g - 1)
                for k in range(KC):
                    if j == 0 and k % 8 == 0:
                        w_wait(n + k // 8)
                    off = (k % 8) * BLK + j * P
                    last = mm(bank[1 + (g + 1) % 2][:, 0:T], ring[:, (n + k // 8) % 4, off:off + P], hT[:, k, :],
                              k == 0, k == KC - 1)
                    if j == 3 and k == 7:
                        last.then_inc(w_used, 1)
                last.then_inc(conv_acc, 1)
                for _ in range(2):
                    if events < 4 * (KC + 1):
                        event(events)
                        events += 1
                if 1 <= g <= NT:
                    turn_qk(g - 1)
                if 0 <= g - 4 < 2 * NH:
                    scores(g - 4)
                if 0 <= g - 5 < 2 * NH:
                    turn_prob(g - 5)
                if 0 <= g - 6 < 2 * NH:
                    values(g - 6)
                if g == 22:
                    pe.wait_ge(osq_added, 2 * NH)
                    mm(bank[3][:, 0:T], ones, ssum[0], True, True).then_inc(sums_done, 1)
            pe.wait_ge(csq_added, CCH)
            mm(bank[4][:, 0:T], ones, ssum[1], True, True).then_inc(sums_done, 1)

            with pe.Fori(0, 2) as i:
                for c in range(8):
                    n = N_ADA1 + N_IN + c // 4 * 2
                    if c < 2:
                        pe.wait_ge(conv_out, 23 + c)
                    if c >= 2:
                        pe.wait_ge(x1_ready, 8 * i + (c - 1))
                    for k in range(KC):
                        if c == 0:
                            pe.wait_ge(mix_ready, k + 1)
                        if c % 4 == 0 and k % 8 == 0:
                            m = n + k // 8
                            pe.wait_ge(w_landed[m % 4], 16 * i + 16 * (m // 4 + 1))
                        off = (k % 8) * BLK + (c % 4) * P
                        last = mm(bank[1 + (c + 1) % 2][:, 0:T], ring[:, (n + k // 8) % 4, off:off + P], mixT[:, k, :],
                                  k == 0, k == KC - 1)
                        if c % 4 == 3 and k == 7:
                            last.then_inc(w_used, 1)
                    last.then_inc(out_acc, 1)
                pe.wait_ge(x1_ready, 8 * i + 8)
            pe.wait_ge(sq2_added, KC)
            mm(bank[3][:, 0:T], ones, ssum2, True, True).then_inc(sums_done, 1)

            pe.wait_ge(wr_in, 16)
            pe.wait_ge(std_ready, 6)
            for k in range(KC):
                pe.wait_ge(h2_ready, k + 1)
                for t in range(NT):
                    last = mm(bank[4][:, t * NE:(t + 1) * NE], hT[:, k, t * P:(t + 1) * P], wr[:, k, :],
                              k == 0 and t == 0, k == KC - 1)
            last.then_inc(logits_done, 1)

            def rows_free(g):
                if g >= 4:
                    pe.wait_ge(rows_out, g - 3)

            def rows_src(g, j):
                return hT[:, g % 4 * 4 + j, g // 4 * P:(g // 4 + 1) * P]
            rows_banks = [bank[5], bank[6], bank[7], bank[1]]
            turn_groups(range(4), rows_src, rows_banks, rows_turned, rows_free)
            pe.wait_ge(aff_ready, 1)
            for t in range(NT):
                last = nc.tensor.transpose(bank[3][0:NE, t * P:(t + 1) * P], lg[:, t, :], ident[:, :])
            last.then_inc(aff_turned, 1)
            turn_groups(range(4, 12), rows_src, rows_banks, rows_turned, rows_free)
            pe.wait_ge(rank_ready, 1)
            for t in range(NT):
                last = nc.tensor.transpose(bank[4][:, t * NE:(t + 1) * NE], rank[:, t * P:(t + 1) * P], ident[0:NE, 0:NE])
            last.then_inc(rank_turned, 1)

            def gather(i):
                pe.wait_ge(pick_ready, i + 1)
                for q in range(4):
                    for kk in range(4):
                        k = 4 * q + kk
                        for t in range(NT):
                            last = mm(bank[4 + q][:, kk * PW:(kk + 1) * PW], h2_rows[:, t, k * P:(k + 1) * P],
                                      pick[:, t * PW:(t + 1) * PW], t == 0, t == NT - 1)
                    last.then_inc(gathered, 1)

            def send(i):
                for s in range(8):
                    if s >= 2:
                        pe.wait_ge(added, 16 * i + (2 * s - 2))
                    for e in range(2):
                        for half in range(2):
                            rows = slice(ES * half, ES * half + ES)
                            last = mm(bank[4 + (2 * s + half) % 4][:, 0:T], y_sb[e][rows, s * P:(s + 1) * P],
                                      giveT[e][rows, :], e == 0, e == 1)
                            if e == 1:
                                last.then_inc(sent, 1)

            pe.wait_ge(rows_out, 12)
            pe.wait_ge(blank, 1)
            gather(0)
            with pe.Fori(0, PAIRS) as i:
                for q in range(PER_PAIR):
                    what, e = MATS[q // 4]
                    part, slot = q % 4, ORDER[q % RING]
                    if part == 0 and what == "g":
                        if e == 0:
                            pe.wait_ge(xs_dve, 2 * i + 2)
                            pe.wait_ge(xs_act, 2 * i + 2)
                        pe.wait_ge(sil_ready, 2 * i + (e + FREE))
                    if part == 0 and what == "u":
                        pe.wait_ge(act_ready, 2 * i + (e + FREE))
                    if part == 0 and what == "d":
                        if e == 1:
                            gather(i + 1)
                            pe.wait_ge(xs_act, 2 * i + 3)
                        pe.wait_ge(added, 16 * i + 16)
                        pe.wait_ge(act_ready, 2 * i + (e + 1 + FREE))
                        for j in range(4):
                            last = nc.tensor.transpose(bank[4][:, j * P:(j + 1) * P], act[:, j * P:(j + 1) * P], ident[:, :])
                        last.then_inc(act_turned, 1)
                        pe.wait_ge(y_out, 2 * i + (e + FREE))
                        pe.wait_ge(giveT_ready, 2 * i + 2)
                        pe.wait_ge(actT_ready, 2 * i + (e + 1))
                    pe.wait_ge(moe_landed[slot], 48 * i + 16 * (q // RING + 1))
                    if what == "d":
                        for ff in range(2):
                            f = 2 * part + ff
                            rows = actT[:, (f % 4) * P + (f // 4) * ES:(f % 4) * P + (f // 4 + 1) * ES]
                            for lower in range(2):
                                for half in range(2):
                                    off = ff * D + half * 2 * BLK + lower * BLK
                                    last = mm(bank[2 + lower][ES * half:ES * half + ES, :], rows,
                                              ring[:, slot, off:off + BLK], f == 0, f == FC - 1)
                    else:
                        for kk in range(4):
                            k = 4 * part + kk
                            for half in range(2):
                                off = kk * FF + half * BLK
                                last = mm(bank[0 if what == "g" else 1][ES * half:ES * half + ES, :],
                                          xs[:, k, e * ES:(e + 1) * ES], ring[:, slot, off:off + BLK], k == 0, k == KC - 1)
                    last.then_inc(moe_used, 1)
                    if q == 7:
                        pe.wait_ge(y_out, 2 * i + FREE)
                        send(i)
                        pe.wait_ge(give_ready, i + 1)
                        for e in range(2):
                            for t in range(NT):
                                col = (2 * t + e) * P
                                last = nc.tensor.transpose(bank[2 + e][:, t * P:(t + 1) * P], give[:, col:col + P], ident[:, :])
                            last.then_inc(give_turned, 1)
            pe.wait_ge(xs_dve, 2 * PAIRS + 2)
            pe.wait_ge(xs_act, 2 * PAIRS + 2)
            pe.wait_ge(y_out, 2 * PAIRS + FREE)
            send(PAIRS)

            pe.wait_ge(added, 16 * (PAIRS + 1))

            def last_free(g):
                if g >= 4:
                    pe.wait_ge(last_act if g % 2 else last_dve, (g - 4) // 2 + 1)
            turn_groups(range(12), lambda g, j: xT[:, g % 4 * 4 + j, g // 4 * P:(g // 4 + 1) * P], bank[0:4], last_turned, last_free)

        @block.scalar
        def _(act_e):
            a = act_e
            ch = Chain(a, act_chain)

            def copy(out, in_):
                return nc.scalar.activation(out, in_, ACT.Copy)

            a.dma_start(ident[:, :], consts[:, C_ID:C_ID + P]).then_inc(small_in, 16)
            a.dma_start(rope, consts[:, C_ROPE:C_ROPE + 256]).then_inc(small_in, 16)
            a.dma_start(iota[:, :], consts[:, C_IOTA:C_IOTA + ES]).then_inc(small_in, 16)
            for src, row, n in ((c, V_C, 16), (c_ctx.rearrange("(a d) -> a d", a=1), V_CTX, 16), (g_norm1, V_G1, 16),
                                (g_norm2, V_G2, 16), (g_attn_out, V_GA, AC), (g_conv_out, V_GC, CCH)):
                a.dma_start(vec_rows[row:row + n, :], src[0].rearrange("(k p) -> k p", p=P)).then_inc(small_in, 16)
            a.dma_start(vec_rows[V_TAP:V_ALL, :], conv_w[0].rearrange("w (k p) -> (w k) p", p=P)).then_inc(small_in, 16)
            a.dma_start(bias_rows, b_ada[0].rearrange("(k p) -> k p", p=P)).then_inc(small_in, 16)
            a.dma_start(kc, cache_k[0, 0].rearrange("s h d -> s (h d)")).then_inc(cache_in, 16)
            a.dma_start(vc, cache_v[0, 0].rearrange("s h d -> s (h d)")).then_inc(cache_in, 16)
            a.dma_start(gqk[:, 0:HD], g_q[0].partition_broadcast(P)).then_inc(cache_in, 16)
            a.dma_start(gqk[:, HD:2 * HD], g_k[0].partition_broadcast(P)).then_inc(cache_in, 16)
            a.dma_start(wr, w_router[0].rearrange("(k p) e -> p k e", p=P)).then_inc(wr_in, 16)

            a.wait_ge(vec_ready, 1)
            a.wait_ge(ada_free, 2)
            nc.scalar.activation(cond[:, :, 0], vecT[:, V_CTX:V_CTX + KC], ACT.Silu)
            nc.scalar.activation(cond[:, :, 1], vecT[:, V_C:V_C + KC], ACT.Silu).then_inc(cond_ready, 1)

            for g in range(1, 12, 2):
                a.wait_ge(x_turned, g + 1)
                t, kk = g // 4, g % 4 * 4
                copy(xT[:, kk:kk + 4, t * P:(t + 1) * P], bank[4 + g % 4][:, :].rearrange("p (j t) -> p j t", j=4))\
                    .then_inc(x_out_act, 1)
            a.wait_ge(x_out_act, 6)
            a.wait_ge(x_out_dve, 6)
            for k in range(KC):
                if k >= 2:
                    a.wait_ge(sq_added, k - 1)
                nc.scalar.activation(sq[k % 2], xT[:, k, :], ACT.Square).then_inc(sq_ready, 1)

            roots = [0]

            def root(ap):
                roots[0] += 1
                a.wait_ge(var_ready, roots[0])
                nc.scalar.activation(ap, ap, ACT.Sqrt).then_inc(std_ready, 1)

            root(rstd[0])

            a.wait_ge(gains_ready, 1)
            for k in range(1, KC, 2):
                for n, (lo, hi) in enumerate(COLS):
                    last = nc.scalar.activation(hT[:, k, lo:hi], hT[:, k, lo:hi], ACT.Identity,
                                                scale=gain[:, 0, k, n:n + 1], bias=mod3[:, k, n:n + 1])
                last.then_inc(h_act, 1)

            for b in range(3):
                for t in range(NT):
                    g = NT * b + t
                    a.wait_ge(qkv_acc, g + 1)
                    dst = kv_rows[:, t, :] if b == 2 else q_rows[:, t, b * BLK:(b + 1) * BLK]
                    copy(dst, bank[1 + g % 2][:, :]).then_inc(qkv_out, 1)

            for g in range(24):
                b, j = g // 4, g % 4
                if g < NT:
                    root(stat[:, 0:10])
                if g == 1:
                    a.wait_ge(qk_ready, 1)
                    a.dma_start(state_k[0, 0].rearrange("s h d -> s (h d)"), kv_rows[:, 0, 0:D_KV]).then_inc(state_out, 16)
                    a.dma_start(state_v[0, 0].rearrange("s h d -> s (h d)"), kv_rows[:, 0, D_KV:2 * D_KV]).then_inc(state_out, 16)
                if 1 <= g <= NT:
                    t = g - 1
                    a.wait_ge(qk_turned, g)
                    copy(qT[:, 0:4, t * P:(t + 1) * P], bank[5][:, :].rearrange("p (h t) -> p h t", h=4))
                    copy(qT[:, 4:8, t * P:(t + 1) * P], bank[6][:, :].rearrange("p (h t) -> p h t", h=4))
                    if t == 0:
                        copy(kT[:, :, P:2 * P], bank[7][:, 2 * P:4 * P].rearrange("p (h t) -> p h t", h=2))
                    at_col = 0 if t == 0 else (1 + t) * P
                    copy(kT[:, :, at_col:at_col + P], bank[7][:, 0:2 * P].rearrange("p (h t) -> p h t", h=2))\
                        .then_inc(qkT_ready, 1)
                n = g - 4
                if 0 <= n < 2 * NH:
                    tiles, nk = (1, 1) if n < NH else (2, 3)
                    a.wait_ge(max_ready, n + 1)
                    if n:
                        a.wait_ge(prob_turned, n)
                    for i in range(tiles):
                        last = nc.scalar.activation(prob[:, i, 0:nk * P], bank[3 + i][:, 0:nk * P], ACT.Exp,
                                                    scale=SCALE, bias=stat[:, 12 + i:13 + i], accum_out=stat[:, 14 + i:15 + i])
                    last.then_inc(exp_done, 1)
                n = g - 5
                if 0 <= n < 2 * NH:
                    a.wait_ge(prob_turned, n + 1)
                    if n:
                        a.wait_ge(o_done, n)
                    if n < NH:
                        last = copy(probT[:, 0, 0:P], bank[5][:, 0:P])
                    else:
                        copy(probT[:, 0:2, :], bank[5][:, :].rearrange("p (j t) -> p j t", j=2))
                        last = copy(probT[:, 2, :], bank[6][:, 0:T_LAT])
                    last.then_inc(probT_ready, 1)
                n = g - 6
                if 0 <= n < 2 * NH:
                    lo, hi = COLS[0 if n < NH else 1]
                    a.wait_ge(o_out, n + 1)
                    if n:
                        a.wait_ge(osq_added, n)
                    nc.scalar.activation(sq[0][:, lo:hi], mixT[:, n % NH, lo:hi], ACT.Square).then_inc(osq_ready, 1)
                if b % 3 == 2:
                    m = b // 3 * 4 + j
                    a.wait_ge(conv_out, g + 1)
                    if m:
                        a.wait_ge(csq_added, m)
                    nc.scalar.activation(sq[1], mixT[:, AC + m, :], ACT.Square).then_inc(csq_ready, 1)
                if g == 22:
                    root(rstd[0])
            root(rstd[1])

            with a.Fori(0, 2) as i:
                for c8 in range(8):
                    a.wait_ge(x1_ready, 8 * i + (c8 + 1))
                    if c8 >= 2:
                        a.wait_ge(sq2_added, 8 * i + (c8 - 1))
                    nc.scalar.activation(sq2[c8 % 2].unsqueeze(1), xT[:, bass.ds(8 * i + c8, 1), :], ACT.Square).then_inc(sq2_ready, 1)
                a.wait_ge(sq2_added, 8 * i + 8)
            root(rstd2)
            a.wait_ge(gains_ready, 2)
            for k in range(KC):
                a.wait_ge(h2n_ready, k + 1)
                for n, (lo, hi) in enumerate(COLS):
                    last = nc.scalar.activation(hT[:, k, lo:hi], hT[:, k, lo:hi], ACT.Identity,
                                                scale=gain[:, 1, k, n:n + 1], bias=mod3[:, 3 * KC + k, n:n + 1])
                last.then_inc(h2_ready, 1)
            a.wait_ge(shifted, 1)
            nc.scalar.activation(lg, lg, ACT.Exp).then_inc(exp2_done, 1)
            rows_banks = [bank[5], bank[6], bank[7], bank[1]]
            for g in range(12):
                a.wait_ge(rows_turned, g + 1)
                kk = g % 4 * BLK
                copy(h2_rows[:, g // 4, kk:kk + BLK], rows_banks[g % 4][:, :]).then_inc(rows_out, 1)

            def xs_copy(i):
                for q in (0, 2):
                    a.wait_ge(gathered, 4 * i + (q + 1))
                    copy(xs[:, 4 * q:4 * q + 4, :], bank[4 + q][:, :].rearrange("p (k s) -> p k s", k=4)).then_inc(xs_act, 1)

            xs_copy(0)
            with a.Fori(0, PAIRS) as i:
                def silu(e):
                    a.wait_ge(moe_used, PER_PAIR * i + (4 + 8 * e))
                    a.wait_ge(act_turned, 2 * i + (e + FREE))
                    nc.scalar.activation(act, bank[0][:, :], ACT.Silu).then_inc(sil_ready, 1)

                def rows_copy(e):
                    a.wait_ge(moe_used, PER_PAIR * i + (16 + 8 * e))
                    copy(y_sb[e][:, 0:BANK], bank[2][:, :])
                    copy(y_sb[e][:, BANK:], bank[3][:, :]).then_inc(y_out, 1)

                silu(0)
                for e in range(2):
                    a.wait_ge(give_turned, 2 * i + (e + 1))
                    copy(giveT[e], bank[2 + e][:, 0:T]).then_inc(giveT_ready, 1)
                silu(1)
                rows_copy(0)
                xs_copy(i + 1)
                rows_copy(1)
            for g in range(1, 12, 2):
                a.wait_ge(last_turned, g + 1)
                kk = g % 4 * BLK
                copy(y_rows[:, g // 4, kk:kk + BLK], bank[g % 4][:, :]).then_inc(last_act, 1)

        @block.vector
        def _(v):
            ch = Chain(v, dve_chain)
            tt, ts, stt = nc.vector.tensor_tensor, nc.vector.tensor_scalar, nc.vector.scalar_tensor_tensor
            copy = nc.vector.tensor_copy

            v.wait_ge(vec_turned, 1)
            copy(vecT[:, :], bank[1][:, 0:V_ALL])
            copy(biasT[:, :], bank[2][:, 0:N_MOD * KC]).then_inc(vec_ready, 1)
            for g in range(0, 12, 2):
                v.wait_ge(x_turned, g + 1)
                t, kk = g // 4, g % 4 * 4
                copy(xT[:, kk:kk + 4, t * P:(t + 1) * P], bank[4 + g % 4][:, :].rearrange("p (j t) -> p j t", j=4))\
                    .then_inc(x_out_dve, 1)
            for k in range(KC):
                v.wait_ge(sq_ready, k + 1)
                if k == 0:
                    copy(ssum[0], sq[0]).then_inc(sq_added, 1)
                else:
                    v.wait_ge(sq_added, k)
                    tt(ssum[0], ssum[0], sq[k % 2], ALU.add).then_inc(sq_added, 1)

            roots = [0]

            def invert_root(out, sums, n):
                roots[0] += 1
                ts(out, sums, 1.0 / n, EPS, ALU.mult, ALU.add).then_inc(var_ready, 1)
                v.wait_ge(std_ready, roots[0])
                ch.link(nc.vector.reciprocal(out, out))

            v.wait_ge(sums_done, 1)
            invert_root(rstd[0], bank[3][:, 0:T], D)
            v.wait_ge(x_out_act, 6)
            for k in range(KC):
                last = tt(hT[:, k, :], xT[:, k, :], rstd[0], ALU.mult)
            ch.link(last)

            def mod_out(m):
                v.wait_ge(mod_turned, m + 1)
                src = bank[2 + m if m < 2 else 0][:, :].rearrange("p (c j n) -> p j c n", c=4, j=4)
                four = [P, 4, 4, 2]
                ins = tt(mod3[:, m * KC:(m + 1) * KC, :].rearrange("p (j c) n -> p j c n", j=4), src[:, :, :, 0:2],
                         biasT[:, m * KC:(m + 1) * KC].rearrange("p (j c) -> p j c", j=4).unsqueeze(3).to_broadcast(four), ALU.add)
                ins.then_inc(mod_read, 1)
                v.wait_ge(mod_read, m + 1)

            def gains(which, scale_m, row):
                stt(gain[:, which, :, :], mod3[:, scale_m * KC:(scale_m + 1) * KC, :], 1.0,
                    vecT[:, row:row + KC].unsqueeze(2).to_broadcast([P, KC, 2]), ALU.add, ALU.mult).then_inc(gains_ready, 1)
                v.wait_ge(gains_ready, which + 1)

            v.wait_ge(w_used, N_ADA1)
            for m in range(2):
                copy(mod_rows[m], bank[m][:, :]).then_inc(mod_rows_out, 1)
            for m in range(2):
                mod_out(m)
            gains(0, 1, V_G1)
            for k in range(0, KC, 2):
                for n, (lo, hi) in enumerate(COLS):
                    last = ts(hT[:, k, lo:hi], hT[:, k, lo:hi], gain[:, 0, k, n:n + 1], mod3[:, k, n:n + 1], ALU.mult, ALU.add)
                last.then_inc(h_dve, 1)

            def prep(t):
                q, k = q_rows[:, t, :], kv_rows[:, t, 0:D_KV]
                if t == 0:
                    v.wait_ge(cache_in, 64)
                ch.link(tt(tmp_a, q, q, ALU.mult))
                ch.link(nc.vector.tensor_reduce(stat[:, 0:8], tmp_a.rearrange("p (h d) -> p h d", h=NH), AX_X, ALU.add))
                ch.link(tt(tmp_b[:, 0:D_KV], k, k, ALU.mult))
                ch.link(nc.vector.tensor_reduce(stat[:, 8:10], tmp_b[:, 0:D_KV].rearrange("p (h d) -> p h d", h=NKV), AX_X, ALU.add))
                invert_root(stat[:, 0:10], stat[:, 0:10], HD)
                for rows, nh, s0, g0 in ((q, NH, 0, 0), (k, NKV, 8, HD)):
                    r3 = rows.rearrange("p (h d) -> p h d", h=nh)
                    ch.link(tt(r3, r3, stat[:, s0:s0 + nh].unsqueeze(2).to_broadcast([P, nh, HD]), ALU.mult))
                    last = tt(r3, r3, gqk[:, g0:g0 + HD].unsqueeze(1).to_broadcast([P, nh, HD]), ALU.mult)
                    if t:
                        ch.link(last)
                        half = rows.rearrange("p (h s d) -> p h s d", s=4, d=32)
                        for axis in range(2):
                            x1, x2 = half[:, :, 2 * axis, :], half[:, :, 2 * axis + 1, :]
                            o = (t - 1) * P + axis * 32
                            cos = rope[:, o:o + 32].unsqueeze(1).to_broadcast([P, nh, 32])
                            sin = rope[:, o + 64:o + 96].unsqueeze(1).to_broadcast([P, nh, 32])
                            ta = [tmp_a[:, n * 256:n * 256 + nh * 32].rearrange("p (h d) -> p h d", h=nh) for n in range(4)]
                            tt(ta[0], x1, cos, ALU.mult)
                            tt(ta[1], x2, sin, ALU.mult)
                            tt(ta[2], x1, sin, ALU.mult)
                            ch.link(tt(ta[3], x2, cos, ALU.mult))
                            tt(x1, ta[0], ta[1], ALU.subtract)
                            last = tt(x2, ta[2], ta[3], ALU.add)
                            if (rows is q) or axis == 0:
                                ch.link(last)
                last.then_inc(qk_ready, 1)
                v.wait_ge(qk_ready, t + 1)

            def after_events(lo, hi):
                for n in range(lo, min(hi, 4 * (KC + 1))):
                    m, k = 2 + n // (KC + 1), n % (KC + 1)
                    if k == KC - 1:
                        v.wait_ge(ada_free, 2 + KC * (m - 1))
                        copy(mod_rows[0], bank[0][:, :]).then_inc(mod_rows_out, 1)
                    if k == KC:
                        mod_out(m)

            after_events(0, 9 * 3)
            for g in range(24):
                b, j = g // 4, g % 4
                src = bank[1 + (g + 1) % 2][:, 0:T]
                v.wait_ge(conv_acc, g + 1)
                if b % 3 == 0:
                    copy(cu[:, j, :], src).then_inc(conv_out, 1)
                elif b % 3 == 1:
                    v.wait_ge(conv_out, g - 3)
                    tt(cu[:, j, :], src, cu[:, j, :], ALU.mult).then_inc(conv_out, 1)
                else:
                    m = b // 3 * 4 + j
                    tap = [vecT[:, V_TAP + w * CCH + m:V_TAP + w * CCH + m + 1] for w in range(3)]
                    v.wait_ge(conv_out, g - 3)
                    ch.link(ts(cv, cu[:, j, :], tap[1], None, ALU.mult))
                    for lo, hi in COLS:
                        last = stt(cv[:, lo + 1:hi], cu[:, j, lo:hi - 1], tap[0], cv[:, lo + 1:hi], ALU.mult, ALU.add)
                    ch.link(last)
                    for lo, hi in COLS:
                        last = stt(cv[:, lo:hi - 1], cu[:, j, lo + 1:hi], tap[2], cv[:, lo:hi - 1], ALU.mult, ALU.add)
                    ch.link(last)
                    tt(mixT[:, AC + m, :], src, cv, ALU.mult).then_inc(conv_out, 1)
                after_events(27 + 2 * g, 29 + 2 * g)
                if g < NT:
                    v.wait_ge(qkv_out, 9)
                    prep(g)
                n = g - 4
                if 0 <= n < 2 * NH:
                    tiles, nk = (1, 1) if n < NH else (2, 3)
                    v.wait_ge(score_done, n + 1)
                    for i in range(tiles):
                        last = nc.vector.tensor_reduce(stat[:, 10 + i:11 + i], bank[3 + i][:, 0:nk * P], AX_X, ALU.max)
                    ch.link(last)
                    ts(stat[:, 12:12 + tiles], stat[:, 10:10 + tiles], -SCALE, None, ALU.mult).then_inc(max_ready, 1)
                    v.wait_ge(exp_done, n + 1)
                    ch.link(nc.vector.reciprocal(stat[:, 16:16 + tiles], stat[:, 14:14 + tiles]))
                    for i in range(tiles):
                        last = ts(prob[:, i, 0:nk * P], prob[:, i, 0:nk * P], stat[:, 16 + i:17 + i], None, ALU.mult)
                    last.then_inc(prob_ready, 1)
                n = g - 6
                if 0 <= n < 2 * NH:
                    lo, hi = COLS[0 if n < NH else 1]
                    v.wait_ge(o_done, n + 1)
                    copy(mixT[:, n % NH, lo:hi], bank[7][:, 0:hi - lo]).then_inc(o_out, 1)
                    v.wait_ge(osq_ready, n + 1)
                    if n % NH == 0:
                        copy(ssum[0][:, lo:hi], sq[0][:, lo:hi]).then_inc(osq_added, 1)
                    else:
                        v.wait_ge(osq_added, n)
                        tt(ssum[0][:, lo:hi], ssum[0][:, lo:hi], sq[0][:, lo:hi], ALU.add).then_inc(osq_added, 1)
                if b % 3 == 2:
                    m = b // 3 * 4 + j
                    v.wait_ge(csq_ready, m + 1)
                    if m == 0:
                        copy(ssum[1], sq[1]).then_inc(csq_added, 1)
                    else:
                        v.wait_ge(csq_added, m)
                        tt(ssum[1], ssum[1], sq[1], ALU.add).then_inc(csq_added, 1)
                if g == 22:
                    v.wait_ge(sums_done, 2)
                    invert_root(rstd[0], bank[3][:, 0:T], D_ATTN)
                    for k in range(AC):
                        stt(mixT[:, k, :], mixT[:, k, :], vecT[:, V_GA + k:V_GA + k + 1], rstd[0], ALU.mult, ALU.mult)\
                            .then_inc(mix_ready, 1)
            v.wait_ge(sums_done, 3)
            invert_root(rstd[1], bank[4][:, 0:T], D_CONV)
            for k in range(CCH):
                stt(mixT[:, AC + k, :], mixT[:, AC + k, :], vecT[:, V_GC + k:V_GC + k + 1], rstd[1], ALU.mult, ALU.mult)\
                    .then_inc(mix_ready, 1)

            ch.link(nc.vector.memset(ssum2, 0.0))
            with v.Fori(0, 2) as i:
                for c8 in range(8):
                    v.wait_ge(out_acc, 8 * i + (c8 + 1))
                    k = 8 * i + c8
                    for n, (lo, hi) in enumerate(COLS):
                        xk = xT[:, bass.ds(k, 1), lo:hi]
                        last = stt(xk, bank[1 + (c8 + 1) % 2][:, lo:hi].unsqueeze(1),
                                   mod3[:, bass.ds(k + 2 * KC, 1), n], xk, ALU.mult, ALU.add)
                    last.then_inc(x1_ready, 1)
                    v.wait_ge(sq2_ready, 8 * i + (c8 + 1))
                    tt(ssum2, ssum2, sq2[c8 % 2], ALU.add).then_inc(sq2_added, 1)
                    v.wait_ge(sq2_added, 8 * i + (c8 + 1))

            gains(1, 4, V_G2)
            v.wait_ge(sums_done, 4)
            invert_root(rstd2, bank[3][:, 0:T], D)
            v.wait_ge(x1_ready, KC)
            for k in range(KC):
                tt(hT[:, k, :], xT[:, k, :], rstd2, ALU.mult).then_inc(h2n_ready, 1)

            v.wait_ge(logits_done, 1)
            b3 = bank[4][:, 0:NT * NE].rearrange("p (n e) -> p n e", n=NT)
            ch.link(nc.vector.tensor_reduce(r_small[:, 0:3], b3, AX_X, ALU.max))
            tt(lg, b3, r_small[:, 0:3].unsqueeze(2).to_broadcast([P, NT, NE]), ALU.subtract).then_inc(shifted, 1)
            v.wait_ge(exp2_done, 1)
            ch.link(nc.vector.tensor_reduce(r_small[:, 3:6], lg, AX_X, ALU.add))
            ch.link(nc.vector.reciprocal(r_small[:, 6:9], r_small[:, 3:6]))
            tt(lg, lg, r_small[:, 6:9].unsqueeze(2).to_broadcast([P, NT, NE]), ALU.mult).then_inc(aff_ready, 1)
            nc.vector.memset(affP[:, 6 * PAIRS:], 0.0)
            nc.vector.memset(slotP[:, 6 * PAIRS:], -1.0)
            v.wait_ge(aff_ready, 1)

            def by_pair(ap):
                return ap[:, 0:6 * PAIRS].rearrange("p (i t e) -> p t i e", t=NT, e=2)
            ch.link(copy(by_pair(affP), lg.rearrange("p t (i e) -> p t i e", e=2)))

            v.wait_ge(aff_turned, 1)
            copy(affT, bank[3][0:NE, 0:T])
            ch.link(copy(work, bank[3][0:NE, 0:T]))
            for cap, (lo, hi) in ((CAP_CTX, COLS[0]), (CAP_LAT, COLS[1])):
                for _ in range(cap // 8):
                    ch.link(nc.vector.max(top8, work[:, lo:hi]))
                    ch.link(nc.vector.match_replace(work[:, lo:hi], top8, work[:, lo:hi], -1.0))
            ch.link(ts(mask, work, 0.0, None, ALU.is_lt))
            for first, (lo, hi) in ((0.0, COLS[0]), (float(CAP_CTX), COLS[1])):
                last = nc.vector.tensor_tensor_scan(rank[:, lo:hi], mask[:, lo:hi], affT[:, lo:hi], first, ALU.add, ALU.bypass)
            ch.link(last)
            ch.link(tt(rank, rank, mask, ALU.mult))
            ts(rank, rank, -1.0, None, ALU.add).then_inc(rank_ready, 1)
            v.wait_ge(rank_turned, 1)
            copy(by_pair(slotP), bank[4][:, 0:NT * NE].rearrange("p (t i e) -> p t i e", t=NT, e=2)).then_inc(routed, 1)

            def make(i):
                six = [P, 6, ES]
                pick3 = pick.rearrange("p (a s) -> p a s", a=6)
                tt(pick3, slotP[:, bass.ds(6 * i, 6)].unsqueeze(2).to_broadcast(six),
                   iota[:, :].unsqueeze(1).to_broadcast(six), ALU.is_equal).then_inc(pick_ready, 1)
                v.wait_ge(pick_ready, i + 1)
                for twice in range(2):
                    last = tt(give.rearrange("p (a r s) -> p a r s", a=6, r=2)[:, :, twice, :], pick3,
                              affP[:, bass.ds(6 * i, 6)].unsqueeze(2).to_broadcast(six), ALU.mult)
                last.then_inc(give_ready, 1)

            def xs_copy(i):
                for q in (1, 3):
                    v.wait_ge(gathered, 4 * i + (q + 1))
                    copy(xs[:, 4 * q:4 * q + 4, :], bank[4 + q][:, :].rearrange("p (k s) -> p k s", k=4)).then_inc(xs_dve, 1)

            def add(i):
                for s in range(8):
                    for half in range(2):
                        k = 8 * half + s
                        v.wait_ge(sent, 16 * i + (2 * s + half + 1))
                        for n, (lo, hi) in enumerate(COLS):
                            last = stt(xT[:, k, lo:hi], bank[4 + (2 * s + half) % 4][:, lo:hi], mod3[:, 5 * KC + k, n:n + 1],
                                       xT[:, k, lo:hi], ALU.mult, ALU.add)
                        last.then_inc(added, 1)

            v.wait_ge(routed, 1)
            v.wait_ge(rows_out, 12)
            nc.vector.memset(y_sb[0], 0.0).then_inc(act_ready, 1)
            nc.vector.memset(y_sb[1], 0.0).then_inc(y_out, 1)
            nc.vector.memset(giveT[0], 0.0).then_inc(sil_ready, 1)
            nc.vector.memset(actT, 0.0).then_inc(act_turned, 1)
            nc.vector.memset(giveT[1], 0.0).then_inc(blank, 1)
            make(0)
            xs_copy(0)
            with v.Fori(0, PAIRS) as i:
                for e in range(2):
                    v.wait_ge(sil_ready, 2 * i + (e + 1 + FREE))
                    v.wait_ge(moe_used, PER_PAIR * i + (8 if e == 0 else 20))
                    tt(act, bank[1][:, :], act, ALU.mult).then_inc(act_ready, 1)
                    if e == 0:
                        add(i)
                        v.wait_ge(give_turned, 2 * i + 2)
                        make(i + 1)
                    else:
                        xs_copy(i + 1)
                    v.wait_ge(act_turned, 2 * i + (e + 1 + FREE))
                    copy(actT, bank[4][:, :]).then_inc(actT_ready, 1)
            add(PAIRS)
            for g in range(0, 12, 2):
                v.wait_ge(last_turned, g + 1)
                kk = g % 4 * BLK
                copy(y_rows[:, g // 4, kk:kk + BLK], bank[g % 4][:, :]).then_inc(last_dve, 1)


def constants():
    out = np.zeros((P, C_ALL), np.float32)
    out[:, C_ID:C_ID + P] = np.eye(P, dtype=np.float32)
    half = HD // 2
    inv = (np.float32(10000.0) ** (-np.arange(0, half, 2, dtype=np.float32) / np.float32(half))).astype(np.float32)
    pos = np.arange(T_LAT)
    ang = np.concatenate([(pos // GRID_W).astype(np.float32)[:, None] * inv,
                          (pos % GRID_W).astype(np.float32)[:, None] * inv], axis=1)
    for n in range(T_LAT // P):
        rows = ang[n * P:(n + 1) * P]
        o = C_ROPE + n * P
        out[:, o:o + 64] = np.cos(rows)
        out[:, o + 64:o + 128] = np.sin(rows)
    out[:, C_IOTA:] = np.arange(ES, dtype=np.float32)
    return out


_INS = ["x_prompt", "x_sample", "cache_k", "cache_v", "c", "c_ctx", "w_ada", "b_ada", "g_norm1", "w_in", "g_q", "g_k",
        "conv_w", "g_attn_out", "g_conv_out", "w_out", "g_norm2", "w_router", "w_gate", "w_up", "w_down"]
_OUTS = [(1, T_CTX, D), (1, T_LAT, D), (1, 1, T_CTX, NKV, HD), (1, 1, T_CTX, NKV, HD)]


def kernel(**inputs):
    import concourse.bacc as bacc
    from concourse.bass_utils import run_bass_kernel_spmd

    nc = bacc.Bacc("TRN2", target_bir_lowering=False, num_devices=1)
    arrays, args = {}, []
    for name in _INS + ["consts"]:
        a = constants() if name == "consts" else np.ascontiguousarray(inputs[name])
        arrays[f"in_{name}"] = a
        args.append(nc.dram_tensor(f"in_{name}", a.shape, mybir.dt.from_np(a.dtype), kind="ExternalInput").ap())
    for i, shape in enumerate(_OUTS):
        args.append(nc.dram_tensor(f"out_{i}", shape, F32, kind="ExternalOutput").ap())
    build(nc, *args)
    r = run_bass_kernel_spmd(nc, [arrays], core_ids=[0])
    return tuple(r.results[0][f"out_{i}"] for i in range(len(_OUTS)))
```

```python
from contextlib import ExitStack

import numpy as np

import concourse.bass as bass
from concourse import mybir

F32 = mybir.dt.float32
F32R = mybir.dt.float32r
ALU = mybir.AluOpType
ACT = mybir.ActivationFunctionType
AX_X = mybir.AxisListType.X

P = 128
D = 2048
KC = D // P
T_CTX, T_LAT = 128, 256
T = T_CTX + T_LAT
NT = T // P
HD = 128
NH, NKV = 8, 2
GROUP = NH // NKV
D_ATTN = NH * HD
D_CONV = D - D_ATTN
AC = D_ATTN // P
CCH = D_CONV // P
D_KV = NKV * HD
D_IN = D_ATTN + 2 * D_KV + 3 * D_CONV
N_MOD = 6
NE = 16
FF = D // 2
FC = FF // P
CAP_CTX, CAP_LAT = 2 * T_CTX // NE, 2 * T_LAT // NE
CAP = CAP_CTX + CAP_LAT
PAIRS = NE // 2
ES = 64
PW = 2 * ES
GRID_W = 64
EPS = 1e-6
SCALE = HD ** -0.5
SLOT = 4096
BLK = 512
UC = 256
UNIT = 8 * UC
RAW = 3
PARTS = 2
BANK = 512

COLS = [(0, T_CTX), (T_CTX, T)]

C_ID, C_ROPE, C_IOTA = 0, P, P + 256
C_ALL = C_IOTA + ES

V_C, V_CTX, V_G1, V_G2, V_GA, V_GC, V_TAP = 0, 16, 32, 48, 64, 72, 80
V_ALL = V_TAP + 3 * CCH

MATS = [("g", 0), ("u", 0), ("g", 1), ("d", 0), ("u", 1), ("d", 1)]
PER_PAIR = 4 * len(MATS)
RING = 8
FIRST_BANKS = [1, 2, 5, 6]
FREE = 1
ORDER = [4, 5, 6, 7, 0, 2, 3, 1]


def build(nc, x_prompt, x_sample, cache_k, cache_v, c, c_ctx, w_ada, b_ada, g_norm1, w_in, g_q, g_k, conv_w,
          g_attn_out, g_conv_out, w_out, g_norm2, w_router, w_gate, w_up, w_down, consts,
          y_prompt, y_sample, state_k, state_v):
    with ExitStack() as ctx:
        def sb(name, shape):
            return ctx.enter_context(nc.sbuf_tensor(name, shape, F32))

        def sem(name):
            return ctx.enter_context(nc.semaphore(name))

        def here():
            return -(-nc.sbuf_base // 32) * 32

        ring_at = here()
        ring = sb("ring", [P, RING, SLOT])
        res = sb("res", [P, KC * T])
        hid_at = here()
        hid = sb("hid", [P, KC * T])
        mix_at = here()
        mix = sb("mix", [P, KC * T])

        def parts_at(name, n, at):
            return nc.alloc_sbuf_tensor_at(name, [P, n], F32R, offset=at)

        raw = ring[:, 0:2, :].rearrange("p s n -> p (s n)")[:, 0:RAW * UNIT]
        w_parts = parts_at("w_parts", PARTS * 2 * UNIT, ring_at + 4 * RAW * UNIT)
        h_parts = parts_at("h_parts", 2 * KC * T, ring_at + 4 * 4 * SLOT)
        attn_parts = parts_at("attn_parts", 2 * AC * T, hid_at)
        conv_parts = parts_at("conv_parts", 2 * CCH * T, mix_at)
        hp = h_parts[:, :].rearrange("p (a k t) -> p a k t", a=2, t=T)
        ap = attn_parts[:, :].rearrange("p (a k t) -> p a k t", a=2, t=T)
        cp = conv_parts[:, :].rearrange("p (a k t) -> p a k t", a=2, t=T)

        def w_part(u, part):
            o = (u % PARTS * 2 + part) * UNIT
            return w_parts[:, o:o + UNIT]

        def raw_unit(u):
            return raw[:, u % RAW * UNIT:(u % RAW + 1) * UNIT]

        xT = res[:, :].rearrange("p (k t) -> p k t", k=KC)
        hT = hid[:, :].rearrange("p (k t) -> p k t", k=KC)
        mixT = mix[:, :].rearrange("p (k t) -> p k t", k=KC)
        x_rows = mix[:, :].rearrange("p (n d) -> p n d", n=NT)
        h2_rows = x_rows
        y_rows = x_rows
        xhatT = mixT
        q_rows = mix[:, AC * T:AC * T + NT * D_ATTN].rearrange("p (n d) -> p n d", n=NT)
        qT = mixT[:, 0:AC, :]

        at = [0]

        def piece(n):
            at[0] += n
            assert at[0] <= KC * T
            return hid[:, at[0] - n:at[0]]

        kv_flat = piece(NT * 2 * D_KV)
        kv_rows = kv_flat.rearrange("p (n d) -> p n d", n=NT)
        kT = piece(NKV * 512).rearrange("p (h t) -> p h t", h=NKV)
        kc = piece(D_KV)
        vc = piece(D_KV)
        assert at[0] == AC * T
        prob_flat = piece(2 * T)
        prob = prob_flat.rearrange("p (n t) -> p n t", n=2)
        vec_rows, bias_rows = prob_flat[0:V_ALL, 0:P], prob_flat[0:6 * KC, P:2 * P]
        probT_flat = piece(3 * T_LAT)
        probT = probT_flat.rearrange("p (j t) -> p j t", j=3)
        tmp = hid[:, at[0] - 2 * T - 3 * T_LAT:at[0]]
        gqk = piece(2 * HD)
        at[0] = cu_at = KC * T - 3 * T
        cu_flat = piece(2 * T)
        cu = cu_flat.rearrange("p (j t) -> p j t", j=2)
        cv = piece(T)
        LO_EARLY = (cu_at - AC * T) // T
        sq1 = [probT_flat[:, 0:T], probT_flat[:, T:2 * T]]
        ssum1 = cu_flat[:, 0:T]
        late = ring[:, 3, SLOT // 2:]
        sq = [late[:, 0:T], late[:, T:2 * T]]
        ssum = [late[:, 2 * T:3 * T], late[:, 3 * T:4 * T]]
        mod_rows = [late[:, 4 * T:4 * T + BANK], kv_flat[:, 0:BANK]]
        ada_buf = [ring[:, 7, 0:D], ring[:, 7, D:2 * D]]
        sq2, ssum2 = sq, ssum[0]
        rt = ring[:, 1, :]
        rstd2 = rt[:, 0:T]
        affT, work, mask, rank = (rt[0:NE, n * T:(n + 1) * T] for n in (1, 2, 3, 4))
        lg = rt[:, 5 * T:5 * T + NT * NE].rearrange("p (n e) -> p n e", n=NT)
        r_small = rt[:, 5 * T + 64:5 * T + 64 + 16]
        lg_parts = rt[:, 6 * T:7 * T]
        top8 = rt[0:NE, 5 * T + 96:5 * T + 96 + 8]

        ident = sb("ident", [P, P])
        iota = sb("iota", [P, ES])
        early = sb("early", [P, 32 * KC + KC * NE + P + 256])
        cond = early[:, 0:32 * KC].rearrange("p (k n) -> p k n", k=KC)
        wr = early[:, 32 * KC:32 * KC + KC * NE].rearrange("p (k e) -> p k e", k=KC)
        ones = early[:, 32 * KC + KC * NE:32 * KC + KC * NE + P]
        rope = early[:, 32 * KC + KC * NE + P:]
        give = early[:, 0:9 * ES].rearrange("p (t s) -> p t s", t=NT)
        pick = early[:, 9 * ES:15 * ES]
        vecT = sb("vecT", [P, V_ALL])
        biasT = sb("biasT", [P, N_MOD * KC])
        mod3 = sb("mod", [P, N_MOD * KC, 2])
        gain = sb("gain", [P, 2, KC, 2])
        stat = sb("stat", [P, 32])
        slotP = sb("slotP", [P, 6 * PAIRS + 6])
        affP = sb("affP", [P, 6 * PAIRS + 6])

        moe_at = [0]

        def moe_piece(n):
            moe_at[0] += n
            assert moe_at[0] <= KC * T
            return hid[:, moe_at[0] - n:moe_at[0]]

        xs = moe_piece(KC * PW).rearrange("p (k s) -> p k s", k=KC)
        act = moe_piece(BANK)
        actT = moe_piece(BANK)
        y_sb = [moe_piece(2 * BANK), moe_piece(2 * BANK)]
        giveT = [moe_piece(T), moe_piece(T)]

        psum = ctx.enter_context(nc.psum_tensor("psum", [P, 8, BANK], F32))
        bank = [psum[:, i, :] for i in range(8)]

        small_in, cache_in, wr_in = sem("small_in"), sem("cache_in"), sem("wr_in")
        x_in = [sem(f"x_in{n}") for n in range(NT)]
        w_landed = [sem(f"w_landed{n}") for n in range(4)]
        w_used = sem("w_used")
        raw_landed = [sem(f"raw_landed{n}") for n in range(RAW)]
        hi_ready, lo_ready, unit_used = sem("hi_ready"), sem("lo_ready"), sem("unit_used")
        h_hi, h_parts_ready = sem("h_hi"), sem("h_parts_ready")
        normed, mix_hi = sem("normed"), sem("mix_hi")
        ada_landed = [sem("ada_landed0"), sem("ada_landed1")]
        ada_free = sem("ada_free")
        moe_landed = [sem(f"moe_landed{n}") for n in range(RING)]
        moe_used = sem("moe_used")
        set_up, vec_turned, vec_ready, cond_ready = sem("set_up"), sem("vec_turned"), sem("vec_ready"), sem("cond_ready")
        x_turned, x_out_dve, x_out_act = sem("x_turned"), sem("x_out_dve"), sem("x_out_act")
        sq_ready, sq_added, sums_done = sem("sq_ready"), sem("sq_added"), sem("sums_done")
        var_ready, std_ready = sem("var_ready"), sem("std_ready")
        gains_ready, mod_rows_out, mod_turned, mod_read = sem("gains_ready"), sem("mod_rows_out"), sem("mod_turned"), sem("mod_read")
        h_dve, h_act = sem("h_dve"), sem("h_act")
        qkv_acc, qkv_out = sem("qkv_acc"), sem("qkv_out")
        conv_acc, conv_out = sem("conv_acc"), sem("conv_out")
        qk_ready, qk_turned, qkT_ready = sem("qk_ready"), sem("qk_turned"), sem("qkT_ready")
        score_done, max_ready, exp_done, prob_ready = sem("score_done"), sem("max_ready"), sem("exp_done"), sem("prob_ready")
        prob_turned, probT_ready, o_done, o_out = sem("prob_turned"), sem("probT_ready"), sem("o_done"), sem("o_out")
        osq_ready, osq_added = sem("osq_ready"), sem("osq_added")
        csq_ready, csq_added = sem("csq_ready"), sem("csq_added")
        mix_ready = sem("mix_ready")
        out_acc, x1_ready = sem("out_acc"), sem("x1_ready")
        sq2_ready, sq2_added = sem("sq2_ready"), sem("sq2_added")
        h2n_ready, h2_act, h2_dve = sem("h2n_ready"), sem("h2_act"), sem("h2_dve")
        logits_done, logits_out, logits_turned, shifted, exp2_done, aff_ready = sem("logits_done"), sem("logits_out"), sem("logits_turned"), sem("shifted"), sem("exp2_done"), sem("aff_ready")
        aff_turned, rank_ready, rank_turned, routed = sem("aff_turned"), sem("rank_ready"), sem("rank_turned"), sem("routed")
        rows_turned, rows_out = sem("rows_turned"), sem("rows_out")
        pick_ready, gathered, xs_dve, xs_act = sem("pick_ready"), sem("gathered"), sem("xs_dve"), sem("xs_act")
        give_ready, blank, give_turned, giveT_ready = sem("give_ready"), sem("blank"), sem("give_turned"), sem("giveT_ready")
        sil_ready, act_ready, act_turned, actT_ready = sem("sil_ready"), sem("act_ready"), sem("act_turned"), sem("actT_ready")
        y_out, sent, added = sem("y_out"), sem("sent"), sem("added")
        last_turned, last_out = sem("last_turned"), sem("last_out")
        dve_chain, act_chain = sem("dve_chain"), sem("act_chain")
        state_out, y_stored = sem("state_out"), sem("y_stored")

        ada_rows = w_ada[0]
        in_rows = w_in[0].rearrange("(k p) n -> p k n", p=P)
        out_rows = w_out[0].rearrange("(k p) n -> p k n", p=P)
        gate_rows = w_gate.rearrange("a e d f -> (a e d) f")
        up_rows = w_up.rearrange("a e d f -> (a e d) f")
        down_rows = w_down.rearrange("a e f d -> (a e f) d")

        o_b = D_ATTN + 2 * D_KV
        o_c, o_u = o_b + D_CONV, o_b + 2 * D_CONV
        N_ADA1 = KC
        U_QKV = 2 * o_b // UC
        U_CONV = 2 * 3 * D_CONV // UC
        U_OUT = 2 * D // UC
        U_ALL = U_QKV + U_CONV + U_OUT
        OUT_UNITS = [(0, 0), (1, 0), (0, 1), (1, 1)] + [(b, half) for b in range(2, U_OUT // 2) for half in range(2)]

        DRAINED = [[], [], [0], [1, 2], [3]] + [[s - 1] for s in range(5, U_OUT + 1)]

        class Chain:

            def __init__(self, eng, s):
                self.eng, self.s, self.n, self.base = eng, s, 0, 0

            def link(self, ins):
                self.n += 1
                ins.then_inc(self.s, 1)
                self.eng.wait_ge(self.s, self.base + self.n)

            def enter(self, i, per):
                self.n0, self.per, self.base = self.n, per, i * per

            def leave(self, trips):
                assert self.n - self.n0 == self.per, self.n - self.n0
                self.n, self.base = self.n0 + trips * self.per, 0

        block = ctx.enter_context(nc.Block())

        @block.sync
        def _(sp):
            for n in range(NT):
                src = x_prompt[0] if n == 0 else x_sample[0, (n - 1) * P:n * P, :]
                sp.dma_start(x_rows[:, n, :], src).then_inc(x_in[n], 16)

            sp.wait_ge(small_in, 16 * 11)
            for n in range(4):
                sp.dma_start(ring[:, n, :], ada_rows[n * P:(n + 1) * P, 0:SLOT]).then_inc(w_landed[n], 16)
            with sp.Fori(1, N_ADA1 // 4) as i:
                for n in range(4):
                    sp.wait_ge(w_used, 4 * i + (n - 3))
                    sp.dma_start(ring[:, n, :], ada_rows[bass.ds(i * 4 * P + n * P, P), 0:SLOT]).then_inc(w_landed[n], 16)

            def unit_load(u, src, half, col, more=0):
                if u >= RAW:
                    sp.wait_ge(lo_ready, more + (u - RAW + 1))
                elif u == RAW - 1:
                    sp.wait_ge(w_used, N_ADA1 - 2)
                elif u == 0:
                    sp.wait_ge(w_used, N_ADA1 - 3)
                sp.dma_start(raw_unit(u).rearrange("p (k n) -> p k n", n=UC), src[:, 8 * half:8 * half + 8, bass.ds(col, UC)])\
                    .then_inc(raw_landed[u % RAW], 16)

            for u in range(U_QKV):
                unit_load(u, in_rows, u % 2, u // 2 * UC)
            with sp.Fori(0, D_CONV // UC) as i:
                for j in range(6):
                    unit_load(U_QKV + j, in_rows, j % 2, i * UC + (o_u, o_c, o_b)[j // 2], 6 * i)
            for j, (b, half) in enumerate(OUT_UNITS):
                unit_load(U_QKV + U_CONV + j, out_rows, half, b * UC)

            def expert_load(pair, q):
                what, e = MATS[q // 4]
                part, slot = q % 4, ORDER[q % RING]
                if what == "d":
                    rows = down_rows[bass.ds(pair * 2 * FF + e * FF + part * 256, 256), :]
                else:
                    rows = (gate_rows if what == "g" else up_rows)[bass.ds(pair * 2 * D + e * D + part * 512, 512), :]
                sp.dma_start(ring[:, slot, :].rearrange("p (k n) -> p k n", k=2 if what == "d" else 4),
                             rows.rearrange("(k p) n -> p k n", p=P)).then_inc(moe_landed[slot], 16)

            sp.wait_ge(unit_used, U_QKV + U_CONV)
            for q in range(RING):
                if ORDER[q] == 7:
                    sp.wait_ge(ada_free, 2 + 64)
                if ORDER[q] == 0:
                    sp.wait_ge(lo_ready, U_ALL)
                if ORDER[q] == 2:
                    sp.wait_ge(unit_used, U_ALL)
                if ORDER[q] == 3:
                    sp.wait_ge(sums_done, 4)
                if ORDER[q] == 1:
                    sp.wait_ge(routed, 1)
                expert_load(0, q)
            with sp.Fori(0, PAIRS - 1) as i:
                for j in range(PER_PAIR):
                    sp.wait_ge(moe_used, PER_PAIR * i + (j + 1))
                    expert_load(i + (j + RING) // PER_PAIR, (j + RING) % PER_PAIR)
            for j in range(PER_PAIR - RING):
                sp.wait_ge(moe_used, PER_PAIR * (PAIRS - 1) + j + 1)
                expert_load(PAIRS - 1, j + RING)

            for q in range(4):
                cols = slice(q * BLK, (q + 1) * BLK)
                sp.wait_ge(last_out, NT * (q + 1))
                sp.dma_start(y_prompt[0, :, cols], y_rows[:, 0, cols]).then_inc(y_stored, 16)
                sp.dma_start(y_sample[0, :, cols].rearrange("(n p) d -> p n d", p=P), y_rows[:, 1:NT, cols]).then_inc(y_stored, 16)
            sp.wait_ge(y_stored, 16 * 8)

        @block.gpsimd
        def _(pool):
            nc.gpsimd.memset(ones, 1.0).then_inc(ada_free, 1)
            nc.gpsimd.memset(cond, 0.0).then_inc(ada_free, 1)
            for m in range(2, N_MOD):
                with pool.Fori(0, KC // 2) as i:
                    for j in range(2):
                        pool.wait_ge(ada_free, 2 * i + (KC * (m - 2) + j + 1))
                        pool.dma_start(ada_buf[j], ada_rows[bass.ds(i * 2 * P + j * P, P), m * D:(m + 1) * D])\
                            .then_inc(ada_landed[j], 16)

        @block.tensor
        def _(pe):
            def mm(out, lhsT, rhs, start, stop):
                return nc.tensor.matmul(out, lhsT, rhs, start=start, stop=stop, skip_group_check=True)

            pe.wait_ge(small_in, 16 * 11)
            nc.tensor.transpose(bank[1][:, 0:V_ALL], vec_rows, ident[0:V_ALL, 0:V_ALL])
            nc.tensor.transpose(bank[2][:, 0:N_MOD * KC], bias_rows, ident[0:N_MOD * KC, 0:N_MOD * KC]).then_inc(vec_turned, 1)

            def turn_groups(groups, src, banks, done, free):
                for g in groups:
                    free(g)
                    for j in range(4):
                        last = nc.tensor.transpose(banks[g % len(banks)][:, j * P:(j + 1) * P], src(g, j), ident[:, :])
                    last.then_inc(done, 1)

            def x_free(g):
                if g % 4 == 0:
                    pe.wait_ge(x_in[g // 4], 16)
                if g >= 4:
                    pe.wait_ge(x_out_act if g % 2 else x_out_dve, (g - 4) // 2 + 1)
            turn_groups(range(12), lambda g, j: x_rows[:, g // 4, (g % 4 * 4 + j) * P:(g % 4 * 4 + j + 1) * P],
                        bank[4:8], x_turned, x_free)
            def ada(out, k, weights, first):
                for j in range(4):
                    last = mm(out[32 * j:32 * j + 32, :], cond[:, k, :], weights[:, j * BLK:(j + 1) * BLK], first, k == KC - 1)
                return last

            def turn_mod(out, rows):
                for j in range(4):
                    last = nc.tensor.transpose(out[:, j * P:(j + 1) * P], rows[:, j * P:(j + 1) * P], ident[:, :])
                last.then_inc(mod_turned, 1)

            pe.wait_ge(cond_ready, 1)
            for k in range(N_ADA1):
                pe.wait_ge(w_landed[k % 4], 16 * (k // 4 + 1))
                for m in range(2):
                    last = ada(bank[m], k, ring[:, k % 4, m * D:(m + 1) * D], k == 0)
                last.then_inc(w_used, 1)
                if k == 4:
                    pe.wait_ge(ada_free, 2)
                    pe.wait_ge(sq_added, KC)
                    mm(bank[3][:, 0:T], ones, ssum1, True, True).then_inc(sums_done, 1)
            for m in range(2):
                pe.wait_ge(mod_rows_out, m + 1)
                turn_mod(bank[2 + m], mod_rows[m])

            def event(n):
                m, k = 2 + n // (KC + 1), n % (KC + 1)
                if k < KC:
                    t = KC * (m - 2) + k
                    if k == 0 and m > 2:
                        pe.wait_ge(mod_read, m)
                    pe.wait_ge(ada_landed[t % 2], 16 * (t // 2 + 1))
                    ada(bank[0], k, ada_buf[t % 2], k == 0).then_inc(ada_free, 1)
                else:
                    pe.wait_ge(mod_rows_out, m + 1)
                    turn_mod(bank[0], mod_rows[0])

            THREE = ((0, 0), (0, 1), (1, 0))

            def weights_tile(u, kk, j, part):
                return w_part(u, part)[:, kk * UC + j * P:kk * UC + (j + 1) * P]

            events = 0
            for u in range(U_QKV):
                b, half = u // 2, u % 2
                pe.wait_ge(lo_ready, u + 1)
                for kk in range(8):
                    k = 8 * half + kk
                    if b == 0:
                        pe.wait_ge(h_parts_ready, k + 1)
                    for t in range(NT):
                        if k == 0 and b >= 2:
                            pe.wait_ge(qkv_out, NT * (b - 2) + t + 1)
                        for wp, hh in THREE:
                            last = mm(bank[1 + NT * (b % 2) + t][:, 0:UC], hp[:, hh, k, t * P:(t + 1) * P],
                                      w_part(u, wp)[:, kk * UC:(kk + 1) * UC], k == 0 and wp + hh == 0, k == KC - 1 and wp == 1)
                        if k == KC - 1 and t < NT - 1:
                            last.then_inc(qkv_acc, 1)
                    if kk == 7:
                        last.then_inc(unit_used, 1)
                    if kk in (2, 6):
                        event(events)
                        events += 1

            def turn_qk(t):
                pe.wait_ge(qk_ready, 5)
                if t:
                    pe.wait_ge(qkT_ready, t)
                else:
                    pe.wait_ge(qkv_out, NT * U_QKV // 2)
                for h in range(NH):
                    nc.tensor.transpose(bank[5 + h // 4][:, (h % 4) * P:(h % 4 + 1) * P],
                                        q_rows[:, t, h * HD:(h + 1) * HD], ident[:, :])
                if t == 0:
                    pe.wait_ge(cache_in, 64)
                    for h in range(NKV):
                        nc.tensor.transpose(bank[7][:, (2 + h) * P:(3 + h) * P], kc[:, h * HD:(h + 1) * HD], ident[:, :])
                for h in range(NKV):
                    last = nc.tensor.transpose(bank[7][:, h * P:(h + 1) * P], kv_rows[:, t, h * HD:(h + 1) * HD], ident[:, :])
                last.then_inc(qk_turned, 1)

            def unit(n):
                h = n % NH
                kv = h // GROUP
                v = [kv_rows[:, t, D_KV + kv * HD:D_KV + (kv + 1) * HD] for t in range(NT)]
                if n < NH:
                    return h, [0], kT[:, kv, 0:P], v[0:1]
                return h, [1, 2], kT[:, kv, P:4 * P], [vc[:, kv * HD:(kv + 1) * HD]] + v[1:]

            def scores(n):
                h, tiles, keys, v = unit(n)
                pe.wait_ge(qkT_ready, NT)
                if n:
                    pe.wait_ge(exp_done, n)
                for i, t in enumerate(tiles):
                    last = mm(bank[3 + i][:, 0:len(v) * P], qT[:, h, t * P:(t + 1) * P], keys, True, True)
                last.then_inc(score_done, 1)

            def turn_prob(n):
                h, tiles, keys, v = unit(n)
                pe.wait_ge(prob_ready, n + 1)
                if n:
                    pe.wait_ge(probT_ready, n)
                for j in range(len(v)):
                    for i in range(len(tiles)):
                        last = nc.tensor.transpose(bank[5 + j // 2][:, (2 * (j % 2) + i) * P:(2 * (j % 2) + i + 1) * P],
                                                   prob[:, i, j * P:(j + 1) * P], ident[:, :])
                last.then_inc(prob_turned, 1)

            def values(n):
                h, tiles, keys, v = unit(n)
                w = len(tiles) * P
                pe.wait_ge(probT_ready, n + 1)
                if n:
                    pe.wait_ge(o_out, n)
                for j, vj in enumerate(v):
                    last = mm(bank[7][:, 0:w], vj, probT[:, j, 0:w], j == 0, j == len(v) - 1)
                last.then_inc(o_done, 1)

            def half_chunk(u, j, half, values, ready=None, out=None):
                out = out or 1 + j
                for kk in range(8):
                    k = 8 * half + kk
                    if ready:
                        pe.wait_ge(ready, k + 1)
                    for wp, hh in THREE:
                        last = mm(bank[out][:, 0:T], weights_tile(u, kk, j, wp), values(hh, k),
                                  k == 0 and wp + hh == 0, k == KC - 1 and wp == 1)
                return last

            for s in range(U_CONV):
                u, g = U_QKV + s, s // 2 * 2
                pe.wait_ge(lo_ready, u + 1)
                for j in range(2):
                    if s == 0:
                        pe.wait_ge(qkv_out, NT * 4 + j + 1)
                    elif s % 2 == 0:
                        pe.wait_ge(conv_out, g + j - 1)
                    last = half_chunk(u, j, s % 2, lambda hh, k: hp[:, hh, k, :])
                    if j == 1:
                        last.then_inc(unit_used, 1)
                    elif s % 2:
                        last.then_inc(conv_acc, 1)
                    if events < 4 * (KC + 1):
                        event(events)
                        events += 1
                if s < NT:
                    turn_qk(s)
                if 0 <= s - 3 < 2 * NH:
                    scores(s - 3)
                if 0 <= s - 4 < 2 * NH:
                    turn_prob(s - 4)
                if 0 <= s - 5 < 2 * NH:
                    values(s - 5)
                if s == 21:
                    pe.wait_ge(osq_added, 2 * NH)
                    mm(bank[3][:, 0:T], ones, ssum[0], True, True).then_inc(sums_done, 1)

            def mixed(hh, k):
                return ap[:, hh, k, :] if k < AC else cp[:, hh, k - AC, :]

            for n in range(4):
                b, half = OUT_UNITS[n]
                u = U_QKV + U_CONV + n
                pe.wait_ge(lo_ready, u + 1)
                for j in range(2):
                    if n == 0:
                        pe.wait_ge(conv_out, 23 + j)
                    last = half_chunk(u, j, half, mixed, mix_ready if b == 0 and j == 0 else None, FIRST_BANKS[2 * b + j])
                    if j == 1:
                        last.then_inc(unit_used, 1)
                    elif half:
                        last.then_inc(out_acc, 1)
                    if n == 0 and j == 0:
                        pe.wait_ge(csq_added, CCH)
                        mm(bank[4][:, 0:T], ones, ssum[1], True, True).then_inc(sums_done, 1)

            def out_block(b, more):
                for half in range(2):
                    u = U_QKV + U_CONV + 2 * b + half
                    pe.wait_ge(lo_ready, 2 * more + (u + 1))
                    for j in range(2):
                        if half == 0:
                            pe.wait_ge(x1_ready, 2 * more + (2 * b + j - 1))
                        last = half_chunk(u, j, half, mixed)
                        if j == 1:
                            last.then_inc(unit_used, 1)
                        elif half:
                            last.then_inc(out_acc, 1)

            with pe.Fori(0, 3) as i:
                out_block(2, 2 * i)
                out_block(3, 2 * i)
            pe.wait_ge(sq2_added, KC - 2)
            mm(bank[3][:, 0:T], ones, ssum2, True, False)
            pe.wait_ge(sq2_ready, KC - 1)
            mm(bank[3][:, 0:T], ones, sq2[0], False, False)
            pe.wait_ge(sq2_ready, KC)
            mm(bank[3][:, 0:T], ones, sq2[1], False, True).then_inc(sums_done, 1)

            pe.wait_ge(wr_in, 16)
            for k in range(KC):
                if k % 3 < 2:
                    pe.wait_ge(h2_act, k - k // 3 + 1)
                else:
                    pe.wait_ge(h2_dve, k // 3 + 1)
                j = 32 * (k % 4)
                last = mm(bank[4][j:j + NE, 0:T], wr[:, k, :], hT[:, k, :], k < 4, k >= KC - 4)
            last.then_inc(logits_done, 1)

            def rows_free(g):
                if g >= 4:
                    pe.wait_ge(rows_out, g - 3)

            def rows_src(g, j):
                return hT[:, g % 4 * 4 + j, g // 4 * P:(g // 4 + 1) * P]
            rows_banks = [bank[5], bank[6], bank[7], bank[1]]
            turn_groups(range(1), rows_src, rows_banks, rows_turned, rows_free)
            pe.wait_ge(logits_out, 1)
            for t in range(NT):
                last = nc.tensor.transpose(bank[3][:, t * P:(t + 1) * P], lg_parts[:, t * P:(t + 1) * P], ident[:, :])
            last.then_inc(logits_turned, 1)
            turn_groups(range(1, 8), rows_src, rows_banks, rows_turned, rows_free)
            pe.wait_ge(aff_ready, 1)
            for t in range(NT):
                last = nc.tensor.transpose(bank[3][0:NE, t * P:(t + 1) * P], lg[:, t, :], ident[:, :])
            last.then_inc(aff_turned, 1)
            turn_groups(range(8, 12), rows_src, rows_banks, rows_turned, rows_free)
            pe.wait_ge(rank_ready, 1)
            for t in range(NT):
                last = nc.tensor.transpose(bank[4][:, t * NE:(t + 1) * NE], rank[:, t * P:(t + 1) * P], ident[0:NE, 0:NE])
            last.then_inc(rank_turned, 1)

            def gather(i):
                pe.wait_ge(pick_ready, i + 1)
                for q in range(4):
                    for kk in range(4):
                        k = 4 * q + kk
                        for t in range(NT):
                            last = mm(bank[4 + q][:, kk * PW:(kk + 1) * PW], h2_rows[:, t, k * P:(k + 1) * P],
                                      pick[:, t * PW:(t + 1) * PW], t == 0, t == NT - 1)
                    last.then_inc(gathered, 1)

            def send(i, lo=0, hi=KC):
                for k in range(lo, hi):
                    if k >= 4:
                        pe.wait_ge(added, 16 * i + (k - 3))
                    mm(bank[4 + k % 4][:, 0:T], y_sb[k // 8][:, k % 8 * P:(k % 8 + 1) * P], giveT[k // 8], True, True)\
                        .then_inc(sent, 1)

            pe.wait_ge(rows_out, 12)
            gather(0)
            pe.wait_ge(blank, 1)
            with pe.Fori(0, PAIRS) as i:
                for q in range(PER_PAIR):
                    what, e = MATS[q // 4]
                    part, slot = q % 4, ORDER[q % RING]
                    if part == 0 and what == "g":
                        if e == 0:
                            pe.wait_ge(xs_dve, 2 * i + 2)
                            pe.wait_ge(xs_act, 2 * i + 2)
                        pe.wait_ge(sil_ready, 2 * i + (e + FREE))
                    if part == 0 and what == "u":
                        pe.wait_ge(act_ready, 2 * i + (e + FREE))
                    if part == 0 and what == "d":
                        if e == 1:
                            gather(i + 1)
                            pe.wait_ge(xs_act, 2 * i + 3)
                        pe.wait_ge(added, 16 * i + 16)
                        pe.wait_ge(act_ready, 2 * i + (e + 1 + FREE))
                        for j in range(4):
                            last = nc.tensor.transpose(bank[4][:, j * P:(j + 1) * P], act[:, j * P:(j + 1) * P], ident[:, :])
                        last.then_inc(act_turned, 1)
                        pe.wait_ge(y_out, 2 * i + (e + FREE))
                        pe.wait_ge(giveT_ready, 2 * i + 2)
                        pe.wait_ge(actT_ready, 2 * i + (e + 1))
                    pe.wait_ge(moe_landed[slot], 48 * i + 16 * (q // RING + 1))
                    if what == "d":
                        for ff in range(2):
                            f = 2 * part + ff
                            rows = actT[:, (f % 4) * P + (f // 4) * ES:(f % 4) * P + (f // 4 + 1) * ES]
                            for lower in range(2):
                                for half in range(2):
                                    off = ff * D + half * 2 * BLK + lower * BLK
                                    row = ES * (half ^ e)
                                    last = mm(bank[2 + lower][row:row + ES, :], rows,
                                              ring[:, slot, off:off + BLK], f == 0, f == FC - 1)
                    else:
                        for kk in range(4):
                            k = 4 * part + kk
                            for half in range(2):
                                off = kk * FF + half * BLK
                                last = mm(bank[0 if what == "g" else 1][ES * half:ES * half + ES, :],
                                          xs[:, k, e * ES:(e + 1) * ES], ring[:, slot, off:off + BLK], k == 0, k == KC - 1)
                    last.then_inc(moe_used, 1)
                    if q == 7:
                        pe.wait_ge(y_out, 2 * i + FREE)
                        send(i)
                        pe.wait_ge(give_ready, i + 1)
                        for e in range(2):
                            for t in range(NT):
                                last = nc.tensor.transpose(bank[2 + e][:, t * P:(t + 1) * P], give[:, t, e * ES:e * ES + P], ident[:, :])
                            last.then_inc(give_turned, 1)
            pe.wait_ge(xs_dve, 2 * PAIRS + 2)
            pe.wait_ge(xs_act, 2 * PAIRS + 2)
            pe.wait_ge(y_out, 2 * PAIRS + FREE)

            def turn_result(q):
                pe.wait_ge(added, 16 * PAIRS + 4 * (q + 1))
                for t in range(NT):
                    g = NT * q + t
                    if g >= 4:
                        pe.wait_ge(last_out, g - 3)
                    for j in range(4):
                        last = nc.tensor.transpose(bank[g % 4][:, j * P:(j + 1) * P], xT[:, 4 * q + j, t * P:(t + 1) * P], ident[:, :])
                    last.then_inc(last_turned, 1)

            send(PAIRS, 0, 8)
            turn_result(0)
            send(PAIRS, 8, 12)
            turn_result(1)
            send(PAIRS, 12, 16)
            turn_result(2)
            turn_result(3)

        @block.scalar
        def _(act_e):
            a = act_e
            ch = Chain(a, act_chain)

            def copy(out, in_):
                return nc.scalar.activation(out, in_, ACT.Copy)

            a.dma_start(ident[:, :], consts[:, C_ID:C_ID + P]).then_inc(small_in, 16)
            a.dma_start(rope, consts[:, C_ROPE:C_ROPE + 256]).then_inc(small_in, 16)
            a.dma_start(iota[:, :], consts[:, C_IOTA:C_IOTA + ES]).then_inc(small_in, 16)
            for src, row, n in ((c, V_C, 16), (c_ctx.rearrange("(a d) -> a d", a=1), V_CTX, 16), (g_norm1, V_G1, 16),
                                (g_norm2, V_G2, 16), (g_attn_out, V_GA, AC), (g_conv_out, V_GC, CCH)):
                a.dma_start(vec_rows[row:row + n, :], src[0].rearrange("(k p) -> k p", p=P)).then_inc(small_in, 16)
            a.dma_start(vec_rows[V_TAP:V_ALL, :], conv_w[0].rearrange("w (k p) -> (w k) p", p=P)).then_inc(small_in, 16)
            a.dma_start(bias_rows, b_ada[0].rearrange("(k p) -> k p", p=P)).then_inc(small_in, 16)

            a.wait_ge(vec_ready, 1)
            a.wait_ge(ada_free, 2)
            nc.scalar.activation(cond[:, :, 0], vecT[:, V_CTX:V_CTX + KC], ACT.Silu)
            nc.scalar.activation(cond[:, :, 1], vecT[:, V_C:V_C + KC], ACT.Silu).then_inc(cond_ready, 1)

            for g in range(1, 12, 2):
                a.wait_ge(x_turned, g + 1)
                t, kk = g // 4, g % 4 * 4
                copy(xT[:, kk:kk + 4, t * P:(t + 1) * P], bank[4 + g % 4][:, :].rearrange("p (j t) -> p j t", j=4))\
                    .then_inc(x_out_act, 1)
            a.wait_ge(x_out_act, 6)
            a.wait_ge(x_out_dve, 6)
            for k in range(KC):
                if k >= 2:
                    a.wait_ge(sq_added, k - 1)
                nc.scalar.activation(sq1[k % 2], xT[:, k, :], ACT.Square).then_inc(sq_ready, 1)

            roots = [0]

            def root(ap):
                roots[0] += 1
                a.wait_ge(var_ready, roots[0])
                nc.scalar.activation(ap, ap, ACT.Sqrt).then_inc(std_ready, 1)

            root(ssum1)

            def hi_part(u):
                if u >= PARTS:
                    a.wait_ge(unit_used, u - PARTS + 1)
                a.wait_ge(raw_landed[u % RAW], 16 * (u // RAW + 1))
                copy(w_part(u, 0), raw_unit(u)).then_inc(hi_ready, 1)

            a.wait_ge(w_used, N_ADA1)
            hi_part(0)
            a.wait_ge(gains_ready, 1)
            for k in range(1, KC, 2):
                for n, (lo, hi) in enumerate(COLS):
                    last = nc.scalar.activation(xhatT[:, k, lo:hi], xhatT[:, k, lo:hi], ACT.Identity,
                                                scale=gain[:, 0, k, n:n + 1], bias=mod3[:, k, n:n + 1])
                last.then_inc(h_act, 1)
                a.wait_ge(h_dve, k // 2 + 1)
                copy(hp[:, 0, k - 1, :], xhatT[:, k - 1, :]).then_inc(h_hi, 1)
                a.wait_ge(h_act, k // 2 + 1)
                copy(hp[:, 0, k, :], xhatT[:, k, :]).then_inc(h_hi, 1)
                if k == 7:
                    hi_part(1)

            a.dma_start(kc, cache_k[0, 0].rearrange("s h d -> s (h d)")).then_inc(cache_in, 16)
            a.dma_start(vc, cache_v[0, 0].rearrange("s h d -> s (h d)")).then_inc(cache_in, 16)
            a.dma_start(gqk[:, 0:HD], g_q[0].partition_broadcast(P)).then_inc(cache_in, 16)
            a.dma_start(gqk[:, HD:2 * HD], g_k[0].partition_broadcast(P)).then_inc(cache_in, 16)
            a.dma_start(wr, w_router[0].rearrange("(k p) e -> p k e", p=P)).then_inc(wr_in, 16)

            for u in range(U_QKV):
                if u:
                    hi_part(u + 1)
                if u and u % 2 == 0:
                    root(stat[:, 0:2 * NT])
                if u % 2:
                    b = u // 2
                    for t in range(NT):
                        if t < NT - 1:
                            a.wait_ge(qkv_acc, (NT - 1) * b + t + 1)
                        else:
                            a.wait_ge(unit_used, u + 1)
                        dst = kv_rows[:, t, (b - 4) * UC:(b - 3) * UC] if b >= 4 else q_rows[:, t, b * UC:(b + 1) * UC]
                        copy(dst, bank[1 + NT * (b % 2) + t][:, 0:UC]).then_inc(qkv_out, 1)

            def csq(m):
                a.wait_ge(conv_out, m // 2 * 6 + m % 2 + 5)
                if m:
                    a.wait_ge(csq_added, m)
                nc.scalar.activation(sq[1], mixT[:, AC + m, :], ACT.Square).then_inc(csq_ready, 1)

            for s in range(U_CONV + 1):
                hi_part(U_QKV + s + 1)
                if s == 0:
                    a.wait_ge(qk_ready, 5)
                    a.wait_ge(qkv_out, NT * U_QKV // 2)
                    a.dma_start(state_k[0, 0].rearrange("s h d -> s (h d)"), kv_rows[:, 0, 0:D_KV]).then_inc(state_out, 16)
                    a.dma_start(state_v[0, 0].rearrange("s h d -> s (h d)"), kv_rows[:, 0, D_KV:2 * D_KV]).then_inc(state_out, 16)
                if 0 <= s - 1 < NT:
                    t = s - 1
                    a.wait_ge(qk_turned, t + 1)
                    copy(qT[:, 0:4, t * P:(t + 1) * P], bank[5][:, :].rearrange("p (h t) -> p h t", h=4))
                    copy(qT[:, 4:8, t * P:(t + 1) * P], bank[6][:, :].rearrange("p (h t) -> p h t", h=4))
                    if t == 0:
                        copy(kT[:, :, P:2 * P], bank[7][:, 2 * P:4 * P].rearrange("p (h t) -> p h t", h=2))
                    at_col = 0 if t == 0 else (1 + t) * P
                    copy(kT[:, :, at_col:at_col + P], bank[7][:, 0:2 * P].rearrange("p (h t) -> p h t", h=2))\
                        .then_inc(qkT_ready, 1)
                n = s - 4
                if 0 <= n < 2 * NH:
                    tiles, nk = (1, 1) if n < NH else (2, 3)
                    a.wait_ge(max_ready, n + 1)
                    if n:
                        a.wait_ge(prob_turned, n)
                    for i in range(tiles):
                        last = nc.scalar.activation(prob[:, i, 0:nk * P], bank[3 + i][:, 0:nk * P], ACT.Exp,
                                                    scale=SCALE, bias=stat[:, 12 + i:13 + i], accum_out=stat[:, 14 + i:15 + i])
                    last.then_inc(exp_done, 1)
                n = s - 5
                if 0 <= n < 2 * NH:
                    a.wait_ge(prob_turned, n + 1)
                    if n:
                        a.wait_ge(o_done, n)
                    if n < NH:
                        last = copy(probT[:, 0, 0:P], bank[5][:, 0:P])
                    else:
                        copy(probT[:, 0:2, :], bank[5][:, :].rearrange("p (j t) -> p j t", j=2))
                        last = copy(probT[:, 2, :], bank[6][:, 0:T_LAT])
                    last.then_inc(probT_ready, 1)
                n = s - 6
                if 0 <= n < 2 * NH:
                    lo, hi = COLS[0 if n < NH else 1]
                    a.wait_ge(o_out, n + 1)
                    if n:
                        a.wait_ge(osq_added, n)
                    nc.scalar.activation(sq[0][:, lo:hi], mixT[:, n % NH, lo:hi], ACT.Square).then_inc(osq_ready, 1)
                if s and s % 6 == 0:
                    csq(s // 3 - 2)
                    csq(s // 3 - 1)
                if s == 22:
                    root(ssum[0])
                    a.wait_ge(state_out, 32)
                    for k in range(AC):
                        a.wait_ge(normed, k + 1)
                        copy(ap[:, 0, k, :], mixT[:, k, :]).then_inc(mix_hi, 1)
            root(ssum[1])
            for k in range(CCH):
                a.wait_ge(normed, AC + k + 1)
                if k == 0:
                    a.wait_ge(mix_ready, AC)
                copy(cp[:, 0, k, :], mixT[:, AC + k, :]).then_inc(mix_hi, 1)
                if k == 1:
                    hi_part(U_QKV + U_CONV + 2)

            def sq2_chunk(c):
                a.wait_ge(x1_ready, c + 1)
                if c >= 2:
                    a.wait_ge(sq2_added, c - 1)
                nc.scalar.activation(sq2[c % 2], xT[:, c, :], ACT.Square).then_inc(sq2_ready, 1)

            for s in range(1, U_OUT + 1):
                if 1 < s < U_OUT - 1:
                    hi_part(U_QKV + U_CONV + s + 1)
                for chunk in DRAINED[s]:
                    sq2_chunk(chunk)
            root(rstd2)
            a.wait_ge(gains_ready, 2)
            for k in range(KC):
                if k % 3 < 2:
                    a.wait_ge(h2n_ready, k + 1)
                    for n, (lo, hi) in enumerate(COLS):
                        last = nc.scalar.activation(hT[:, k, lo:hi], hT[:, k, lo:hi], ACT.Identity,
                                                    scale=gain[:, 1, k, n:n + 1], bias=mod3[:, 3 * KC + k, n:n + 1])
                    last.then_inc(h2_act, 1)
            a.wait_ge(shifted, 1)
            nc.scalar.activation(lg, lg, ACT.Exp).then_inc(exp2_done, 1)
            rows_banks = [bank[5], bank[6], bank[7], bank[1]]
            for g in range(12):
                a.wait_ge(rows_turned, g + 1)
                kk = g % 4 * BLK
                copy(h2_rows[:, g // 4, kk:kk + BLK], rows_banks[g % 4][:, :]).then_inc(rows_out, 1)

            def xs_copy(i):
                for q in (0, 2):
                    a.wait_ge(gathered, 4 * i + (q + 1))
                    copy(xs[:, 4 * q:4 * q + 4, :], bank[4 + q][:, :].rearrange("p (k s) -> p k s", k=4)).then_inc(xs_act, 1)

            xs_copy(0)
            with a.Fori(0, PAIRS) as i:
                def silu(e):
                    a.wait_ge(moe_used, PER_PAIR * i + (4 + 8 * e))
                    a.wait_ge(act_turned, 2 * i + (e + FREE))
                    nc.scalar.activation(act, bank[0][:, :], ACT.Silu).then_inc(sil_ready, 1)

                def rows_copy(e):
                    a.wait_ge(moe_used, PER_PAIR * i + (16 + 8 * e))
                    for half in range(2):
                        row = ES * (half ^ e)
                        last = copy(y_sb[half][row:row + ES, :].rearrange("p (b n) -> p b n", b=2), psum[row:row + ES, 2:4, :])
                    last.then_inc(y_out, 1)

                silu(0)
                for e in range(2):
                    a.wait_ge(give_turned, 2 * i + (e + 1))
                    copy(giveT[e], bank[2 + e][:, 0:T]).then_inc(giveT_ready, 1)
                silu(1)
                rows_copy(0)
                xs_copy(i + 1)
                rows_copy(1)
            for g in range(12):
                a.wait_ge(last_turned, g + 1)
                copy(y_rows[:, g % NT, g // NT * BLK:(g // NT + 1) * BLK], bank[g % 4][:, :]).then_inc(last_out, 1)

        @block.vector
        def _(v):
            ch = Chain(v, dve_chain)
            tt, ts, stt = nc.vector.tensor_tensor, nc.vector.tensor_scalar, nc.vector.scalar_tensor_tensor
            copy = nc.vector.tensor_copy

            v.wait_ge(vec_turned, 1)
            copy(vecT[:, :], bank[1][:, 0:V_ALL])
            copy(biasT[:, :], bank[2][:, 0:N_MOD * KC]).then_inc(vec_ready, 1)
            for g in range(0, 12, 2):
                v.wait_ge(x_turned, g + 1)
                t, kk = g // 4, g % 4 * 4
                copy(xT[:, kk:kk + 4, t * P:(t + 1) * P], bank[4 + g % 4][:, :].rearrange("p (j t) -> p j t", j=4))\
                    .then_inc(x_out_dve, 1)
            for k in range(KC):
                v.wait_ge(sq_ready, k + 1)
                if k == 0:
                    copy(ssum1, sq1[0]).then_inc(sq_added, 1)
                else:
                    v.wait_ge(sq_added, k)
                    tt(ssum1, ssum1, sq1[k % 2], ALU.add).then_inc(sq_added, 1)

            roots = [0]

            def invert_root(out, sums, n):
                roots[0] += 1
                ts(out, sums, 1.0 / n, EPS, ALU.mult, ALU.add).then_inc(var_ready, 1)
                v.wait_ge(std_ready, roots[0])
                ch.link(nc.vector.reciprocal(out, out))

            v.wait_ge(sums_done, 1)
            invert_root(ssum1, bank[3][:, 0:T], D)
            v.wait_ge(x_out_act, 6)
            for k in range(KC):
                last = tt(xhatT[:, k, :], xT[:, k, :], ssum1, ALU.mult)
            ch.link(last)

            def lo_part(u):
                v.wait_ge(hi_ready, u + 1)
                tt(w_part(u, 1), raw_unit(u), w_part(u, 0).bitcast(F32), ALU.subtract).then_inc(lo_ready, 1)

            def mod_out(m):
                v.wait_ge(mod_turned, m + 1)
                src = bank[2 + m if m < 2 else 0][:, :].rearrange("p (c j n) -> p j c n", c=4, j=4)
                four = [P, 4, 4, 2]
                ins = tt(mod3[:, m * KC:(m + 1) * KC, :].rearrange("p (j c) n -> p j c n", j=4), src[:, :, :, 0:2],
                         biasT[:, m * KC:(m + 1) * KC].rearrange("p (j c) -> p j c", j=4).unsqueeze(3).to_broadcast(four), ALU.add)
                ins.then_inc(mod_read, 1)
                v.wait_ge(mod_read, m + 1)

            def gains(which, scale_m, row):
                stt(gain[:, which, :, :], mod3[:, scale_m * KC:(scale_m + 1) * KC, :], 1.0,
                    vecT[:, row:row + KC].unsqueeze(2).to_broadcast([P, KC, 2]), ALU.add, ALU.mult).then_inc(gains_ready, 1)
                v.wait_ge(gains_ready, which + 1)

            v.wait_ge(w_used, N_ADA1)
            for m in range(2):
                copy(mod_rows[m], bank[m][:, :]).then_inc(mod_rows_out, 1)
            for m in range(2):
                mod_out(m)
            gains(0, 1, V_G1)
            def h_even(k):
                for n, (lo, hi) in enumerate(COLS):
                    last = ts(xhatT[:, k, lo:hi], xhatT[:, k, lo:hi], gain[:, 0, k, n:n + 1], mod3[:, k, n:n + 1], ALU.mult, ALU.add)
                last.then_inc(h_dve, 1)

            h_even(0)
            for k in range(0, KC, 2):
                if k + 2 < KC:
                    h_even(k + 2)
                for kk in (k, k + 1):
                    v.wait_ge(h_hi, kk + 1)
                    tt(hp[:, 1, kk, :], xhatT[:, kk, :], hp[:, 0, kk, :].bitcast(F32), ALU.subtract).then_inc(h_parts_ready, 1)
                if k == 0:
                    lo_part(0)
                if k == 6:
                    lo_part(1)

            def prep(b):
                src, g0 = (q_rows[:, :, b * UC:(b + 1) * UC], 0) if b < 4 else (kv_rows[:, :, 0:D_KV], HD)
                rows = src.rearrange("p t (h d) -> p t h d", d=HD)
                shape = [P, NT, 2, HD]
                if b == 0:
                    v.wait_ge(cache_in, 64)
                v.wait_ge(qkv_out, NT * (b + 1))
                squares = tmp[:, 0:NT * UC].rearrange("p (t h d) -> p t h d", t=NT, d=HD)
                sums = stat[:, 0:2 * NT]
                ch.link(tt(squares, rows, rows, ALU.mult))
                ch.link(nc.vector.tensor_reduce(sums.rearrange("p (t h) -> p t h", t=NT), squares, AX_X, ALU.add))
                invert_root(sums, sums, HD)
                ch.link(tt(rows, rows, sums.rearrange("p (t h) -> p t h", t=NT).unsqueeze(3).to_broadcast(shape), ALU.mult))
                ch.link(tt(rows, rows, gqk[:, g0:g0 + HD].unsqueeze(1).unsqueeze(1).to_broadcast(shape), ALU.mult))
                table = rope.rearrange("p (t x) -> p t x", t=NT - 1)
                four = [P, NT - 1, 2, 32]
                for axis in range(2):
                    x1, x2 = (rows[:, 1:NT, :, 64 * axis + 32 * n:64 * axis + 32 * n + 32] for n in range(2))
                    cos, sin = (table[:, :, o + axis * 32:o + axis * 32 + 32].unsqueeze(2).to_broadcast(four) for o in (0, 64))
                    ta = [tmp[:, n * P:(n + 1) * P].rearrange("p (t h d) -> p t h d", t=NT - 1, d=32) for n in range(4)]
                    tt(ta[0], x1, cos, ALU.mult)
                    tt(ta[1], x2, sin, ALU.mult)
                    tt(ta[2], x1, sin, ALU.mult)
                    ch.link(tt(ta[3], x2, cos, ALU.mult))
                    tt(x1, ta[0], ta[1], ALU.subtract)
                    last = tt(x2, ta[2], ta[3], ALU.add)
                    if axis == 0:
                        ch.link(last)
                last.then_inc(qk_ready, 1)
                v.wait_ge(qk_ready, b + 1)

            def after_events(lo, hi):
                for n in range(lo, min(hi, 4 * (KC + 1))):
                    m, k = 2 + n // (KC + 1), n % (KC + 1)
                    if k == KC - 1:
                        v.wait_ge(ada_free, 2 + KC * (m - 1))
                        copy(mod_rows[0], bank[0][:, :]).then_inc(mod_rows_out, 1)
                    if k == KC:
                        mod_out(m)

            for u in range(U_QKV):
                if u:
                    lo_part(u + 1)
                after_events(2 * u, 2 * u + 2)
                if u and u % 2 == 0:
                    prep(u // 2 - 1)

            def taps(m):
                j = m % 2
                tap = [vecT[:, V_TAP + w * CCH + m:V_TAP + w * CCH + m + 1] for w in range(3)]
                v.wait_ge(conv_out, m // 2 * 6 + m % 2 + 4)
                ch.link(ts(cv, cu[:, j, :], tap[1], None, ALU.mult))
                for lo, hi in COLS:
                    last = stt(cv[:, lo + 1:hi], cu[:, j, lo:hi - 1], tap[0], cv[:, lo + 1:hi], ALU.mult, ALU.add)
                ch.link(last)
                for lo, hi in COLS:
                    last = stt(cv[:, lo:hi - 1], cu[:, j, lo + 1:hi], tap[2], cv[:, lo:hi - 1], ALU.mult, ALU.add)
                ch.link(last)

            def conv_chunk(b, j):
                src = bank[1 + j][:, 0:T]
                if j == 0:
                    v.wait_ge(conv_acc, b + 1)
                else:
                    v.wait_ge(unit_used, U_QKV + 2 * b + 2)
                if b % 3 == 0:
                    copy(cu[:, j, :], src).then_inc(conv_out, 1)
                elif b % 3 == 1:
                    v.wait_ge(conv_out, 2 * b + j - 1)
                    tt(cu[:, j, :], src, cu[:, j, :], ALU.mult).then_inc(conv_out, 1)
                else:
                    m = b // 3 * 2 + j
                    tt(mixT[:, AC + m, :], src, cv, ALU.mult).then_inc(conv_out, 1)
                    if j == 0:
                        taps(m + 1)

            def csq_add(m):
                v.wait_ge(csq_ready, m + 1)
                if m == 0:
                    copy(ssum[1], sq[1]).then_inc(csq_added, 1)
                else:
                    v.wait_ge(csq_added, m)
                    tt(ssum[1], ssum[1], sq[1], ALU.add).then_inc(csq_added, 1)

            def mix_lo(k):
                v.wait_ge(mix_hi, k + 1)
                parts, n = (ap, k) if k < AC else (cp, k - AC)
                tt(parts[:, 1, n, :], mixT[:, k, :], parts[:, 0, n, :].bitcast(F32), ALU.subtract).then_inc(mix_ready, 1)

            for s in range(U_CONV + 1):
                if s and s % 2 == 0:
                    conv_chunk(s // 2 - 1, 1)
                if s == U_CONV:
                    v.wait_ge(conv_out, 24)
                    for k in range(LO_EARLY, AC):
                        mix_lo(k)
                n = s - 4
                if 0 <= n < 2 * NH:
                    tiles, nk = (1, 1) if n < NH else (2, 3)
                    v.wait_ge(score_done, n + 1)
                    for i in range(tiles):
                        last = nc.vector.tensor_reduce(stat[:, 10 + i:11 + i], bank[3 + i][:, 0:nk * P], AX_X, ALU.max)
                    ch.link(last)
                    ts(stat[:, 12:12 + tiles], stat[:, 10:10 + tiles], -SCALE, None, ALU.mult).then_inc(max_ready, 1)
                if s < U_CONV:
                    lo_part(U_QKV + s + 1)
                    after_events(2 * (U_QKV + s), 2 * (U_QKV + s) + 2)
                if 0 <= n < 2 * NH:
                    v.wait_ge(exp_done, n + 1)
                    ch.link(nc.vector.reciprocal(stat[:, 16:16 + tiles], stat[:, 14:14 + tiles]))
                    for i in range(tiles):
                        last = ts(prob[:, i, 0:nk * P], prob[:, i, 0:nk * P], stat[:, 16 + i:17 + i], None, ALU.mult)
                    last.then_inc(prob_ready, 1)
                n = s - 6
                if 0 <= n < 2 * NH:
                    lo, hi = COLS[0 if n < NH else 1]
                    v.wait_ge(o_done, n + 1)
                    copy(mixT[:, n % NH, lo:hi], bank[7][:, 0:hi - lo]).then_inc(o_out, 1)
                    v.wait_ge(osq_ready, n + 1)
                    if n % NH == 0:
                        copy(ssum[0][:, lo:hi], sq[0][:, lo:hi]).then_inc(osq_added, 1)
                    else:
                        v.wait_ge(osq_added, n)
                        tt(ssum[0][:, lo:hi], ssum[0][:, lo:hi], sq[0][:, lo:hi], ALU.add).then_inc(osq_added, 1)
                if s and s % 6 == 0:
                    csq_add(s // 3 - 2)
                    csq_add(s // 3 - 1)
                if s == 22:
                    v.wait_ge(sums_done, 2)
                    invert_root(ssum[0], bank[3][:, 0:T], D_ATTN)
                    for k in range(AC):
                        stt(mixT[:, k, :], mixT[:, k, :], vecT[:, V_GA + k:V_GA + k + 1], ssum[0], ALU.mult, ALU.mult)\
                            .then_inc(normed, 1)
                if s % 6 == 4:
                    taps(s // 6 * 2)
                if s % 2:
                    conv_chunk(s // 2, 0)
                if s == U_CONV - 1:
                    for k in range(LO_EARLY):
                        mix_lo(k)
            lo_part(U_QKV + U_CONV + 1)
            v.wait_ge(sums_done, 3)
            invert_root(ssum[1], bank[4][:, 0:T], D_CONV)
            for k in range(CCH):
                stt(mixT[:, AC + k, :], mixT[:, AC + k, :], vecT[:, V_GC + k:V_GC + k + 1], ssum[1], ALU.mult, ALU.mult)\
                    .then_inc(normed, 1)
                if k:
                    mix_lo(AC + k - 1)
                if k == 2:
                    lo_part(U_QKV + U_CONV + 2)
            mix_lo(KC - 1)

            ch.link(nc.vector.memset(ssum2, 0.0))

            def x1_chunk(c):
                if c % 2 == 0:
                    v.wait_ge(out_acc, c // 2 + 1)
                else:
                    v.wait_ge(unit_used, U_QKV + U_CONV + (3 + c // 2 if c < 4 else c + 1))
                src = bank[FIRST_BANKS[c] if c < 4 else 1 + c % 2]
                for n, (lo, hi) in enumerate(COLS):
                    last = stt(xT[:, c, lo:hi], src[:, lo:hi], mod3[:, 2 * KC + c, n:n + 1], xT[:, c, lo:hi],
                               ALU.mult, ALU.add)
                last.then_inc(x1_ready, 1)

            def sq2_add(c):
                v.wait_ge(sq2_ready, c + 1)
                if c:
                    v.wait_ge(sq2_added, c)
                tt(ssum2, ssum2, sq2[c % 2], ALU.add).then_inc(sq2_added, 1)

            for s in range(1, U_OUT + 1):
                for c in DRAINED[s]:
                    if c % 2:
                        x1_chunk(c)
                if 1 < s < U_OUT - 1:
                    lo_part(U_QKV + U_CONV + s + 1)
                for c in DRAINED[s]:
                    if c % 2 == 0:
                        x1_chunk(c)
                for c in DRAINED[s - 1]:
                    if c < KC - 2:
                        sq2_add(c)

            gains(1, 4, V_G2)
            v.wait_ge(sums_done, 4)
            v.wait_ge(unit_used, U_ALL)
            invert_root(rstd2, bank[3][:, 0:T], D)
            v.wait_ge(x1_ready, KC)
            for k in range(KC):
                tt(hT[:, k, :], xT[:, k, :], rstd2, ALU.mult).then_inc(h2n_ready, 1)
                if k % 3 == 0 and k:
                    kk = k - 1
                    v.wait_ge(h2n_ready, k)
                    for n, (lo, hi) in enumerate(COLS):
                        last = ts(hT[:, kk, lo:hi], hT[:, kk, lo:hi], gain[:, 1, kk, n:n + 1], mod3[:, 3 * KC + kk, n:n + 1],
                                  ALU.mult, ALU.add)
                    last.then_inc(h2_dve, 1)

            v.wait_ge(logits_done, 1)
            copy(lg_parts, bank[4][:, 0:T]).then_inc(logits_out, 1)
            v.wait_ge(logits_turned, 1)
            parts = bank[3][:, 0:T].rearrange("p (t j e) -> p t e j", t=NT, j=4)
            ch.link(nc.vector.tensor_reduce(lg, parts[:, :, 0:NE, :], AX_X, ALU.add))
            ch.link(nc.vector.tensor_reduce(r_small[:, 0:3], lg, AX_X, ALU.max))
            tt(lg, lg, r_small[:, 0:3].unsqueeze(2).to_broadcast([P, NT, NE]), ALU.subtract).then_inc(shifted, 1)
            v.wait_ge(exp2_done, 1)
            ch.link(nc.vector.tensor_reduce(r_small[:, 3:6], lg, AX_X, ALU.add))
            ch.link(nc.vector.reciprocal(r_small[:, 6:9], r_small[:, 3:6]))
            tt(lg, lg, r_small[:, 6:9].unsqueeze(2).to_broadcast([P, NT, NE]), ALU.mult).then_inc(aff_ready, 1)
            nc.vector.memset(affP[:, 6 * PAIRS:], 0.0)
            nc.vector.memset(slotP[:, 6 * PAIRS:], -1.0)
            v.wait_ge(aff_ready, 1)

            def by_pair(ap):
                return ap[:, 0:6 * PAIRS].rearrange("p (i t e) -> p t i e", t=NT, e=2)
            ch.link(copy(by_pair(affP), lg.rearrange("p t (i e) -> p t i e", e=2)))

            v.wait_ge(aff_turned, 1)
            copy(affT, bank[3][0:NE, 0:T])
            ch.link(copy(work, bank[3][0:NE, 0:T]))
            for cap, (lo, hi) in ((CAP_CTX, COLS[0]), (CAP_LAT, COLS[1])):
                for _ in range(cap // 8):
                    ch.link(nc.vector.max(top8, work[:, lo:hi]))
                    ch.link(nc.vector.match_replace(work[:, lo:hi], top8, work[:, lo:hi], -1.0))
            ch.link(ts(mask, work, 0.0, None, ALU.is_lt))
            for first, (lo, hi) in ((0.0, COLS[0]), (float(CAP_CTX), COLS[1])):
                last = nc.vector.tensor_tensor_scan(rank[:, lo:hi], mask[:, lo:hi], affT[:, lo:hi], first, ALU.add, ALU.bypass)
            ch.link(last)
            ch.link(tt(rank, rank, mask, ALU.mult))
            ts(rank, rank, -1.0, None, ALU.add).then_inc(rank_ready, 1)
            v.wait_ge(rank_turned, 1)
            copy(by_pair(slotP), bank[4][:, 0:NT * NE].rearrange("p (t i e) -> p t i e", t=NT, e=2)).then_inc(routed, 1)

            def make(i):
                six = [P, 6, ES]
                pick3 = pick.rearrange("p (a s) -> p a s", a=6)
                tt(pick3, slotP[:, bass.ds(6 * i, 6)].unsqueeze(2).to_broadcast(six),
                   iota[:, :].unsqueeze(1).to_broadcast(six), ALU.is_equal).then_inc(pick_ready, 1)
                v.wait_ge(pick_ready, i + 1)
                aff = affP[:, bass.ds(6 * i, 6)].rearrange("p (t e) -> p t e", e=2)
                by_tile = pick.rearrange("p (t e s) -> p t e s", t=NT, e=2)
                tt(give[:, :, 0:2 * ES].rearrange("p t (e s) -> p t e s", e=2), by_tile,
                   aff.unsqueeze(3).to_broadcast([P, NT, 2, ES]), ALU.mult)
                last = tt(give[:, :, 2 * ES:], by_tile[:, :, 0, :], aff[:, :, 0:1].to_broadcast([P, NT, ES]), ALU.mult)
                last.then_inc(give_ready, 1)

            def xs_copy(i):
                for q in (1, 3):
                    v.wait_ge(gathered, 4 * i + (q + 1))
                    copy(xs[:, 4 * q:4 * q + 4, :], bank[4 + q][:, :].rearrange("p (k s) -> p k s", k=4)).then_inc(xs_dve, 1)

            def add(i):
                for k in range(KC):
                    v.wait_ge(sent, 16 * i + (k + 1))
                    for n, (lo, hi) in enumerate(COLS):
                        last = stt(xT[:, k, lo:hi], bank[4 + k % 4][:, lo:hi], mod3[:, 5 * KC + k, n:n + 1],
                                   xT[:, k, lo:hi], ALU.mult, ALU.add)
                    last.then_inc(added, 1)

            v.wait_ge(routed, 1)
            v.wait_ge(rows_out, 12)
            make(0)
            nc.vector.memset(y_sb[0], 0.0).then_inc(act_ready, 1)
            nc.vector.memset(y_sb[1], 0.0).then_inc(y_out, 1)
            nc.vector.memset(giveT[0], 0.0).then_inc(sil_ready, 1)
            nc.vector.memset(actT, 0.0).then_inc(act_turned, 1)
            nc.vector.memset(giveT[1], 0.0).then_inc(blank, 1)
            xs_copy(0)
            with v.Fori(0, PAIRS) as i:
                for e in range(2):
                    v.wait_ge(sil_ready, 2 * i + (e + 1 + FREE))
                    v.wait_ge(moe_used, PER_PAIR * i + (8 if e == 0 else 20))
                    tt(act, bank[1][:, :], act, ALU.mult).then_inc(act_ready, 1)
                    if e == 0:
                        add(i)
                        v.wait_ge(give_turned, 2 * i + 2)
                        make(i + 1)
                    else:
                        xs_copy(i + 1)
                    v.wait_ge(act_turned, 2 * i + (e + 1 + FREE))
                    copy(actT, bank[4][:, :]).then_inc(actT_ready, 1)
            add(PAIRS)


def constants():
    out = np.zeros((P, C_ALL), np.float32)
    out[:, C_ID:C_ID + P] = np.eye(P, dtype=np.float32)
    half = HD // 2
    inv = (np.float32(10000.0) ** (-np.arange(0, half, 2, dtype=np.float32) / np.float32(half))).astype(np.float32)
    pos = np.arange(T_LAT)
    ang = np.concatenate([(pos // GRID_W).astype(np.float32)[:, None] * inv,
                          (pos % GRID_W).astype(np.float32)[:, None] * inv], axis=1)
    for n in range(T_LAT // P):
        rows = ang[n * P:(n + 1) * P]
        o = C_ROPE + n * P
        out[:, o:o + 64] = np.cos(rows)
        out[:, o + 64:o + 128] = np.sin(rows)
    out[:, C_IOTA:] = np.arange(ES, dtype=np.float32)
    return out


_INS = ["x_prompt", "x_sample", "cache_k", "cache_v", "c", "c_ctx", "w_ada", "b_ada", "g_norm1", "w_in", "g_q", "g_k",
        "conv_w", "g_attn_out", "g_conv_out", "w_out", "g_norm2", "w_router", "w_gate", "w_up", "w_down"]
_OUTS = [(1, T_CTX, D), (1, T_LAT, D), (1, 1, T_CTX, NKV, HD), (1, 1, T_CTX, NKV, HD)]


def kernel(**inputs):
    import concourse.bacc as bacc
    from concourse.bass_utils import run_bass_kernel_spmd

    nc = bacc.Bacc("TRN2", target_bir_lowering=False, num_devices=1)
    arrays, args = {}, []
    for name in _INS + ["consts"]:
        a = constants() if name == "consts" else np.ascontiguousarray(inputs[name])
        arrays[f"in_{name}"] = a
        args.append(nc.dram_tensor(f"in_{name}", a.shape, mybir.dt.from_np(a.dtype), kind="ExternalInput").ap())
    for i, shape in enumerate(_OUTS):
        args.append(nc.dram_tensor(f"out_{i}", shape, F32, kind="ExternalOutput").ap())
    build(nc, *args)
    r = run_bass_kernel_spmd(nc, [arrays], core_ids=[0])
    return tuple(r.results[0][f"out_{i}"] for i in range(len(_OUTS)))
```

```python
from contextlib import ExitStack

import numpy as np

import concourse.bass as bass
from concourse import mybir

F32 = mybir.dt.float32
F32R = mybir.dt.float32r
ALU = mybir.AluOpType
ACT = mybir.ActivationFunctionType
AX_X = mybir.AxisListType.X

P = 128
D = 2048
KC = D // P
T_CTX, T_LAT = 128, 256
T = T_CTX + T_LAT
NT = T // P
HD = 128
NH, NKV = 8, 2
GROUP = NH // NKV
D_ATTN = NH * HD
D_CONV = D - D_ATTN
AC = D_ATTN // P
CCH = D_CONV // P
D_KV = NKV * HD
N_MOD = 6
NE = 16
FF = D // 2
FC = FF // P
CAP_CTX, CAP_LAT = 2 * T_CTX // NE, 2 * T_LAT // NE
CAP = CAP_CTX + CAP_LAT
PAIRS = NE // 2
ES = 64
PW = 2 * ES
assert CAP <= ES
GRID_W = 64
EPS = 1e-6
SCALE = HD ** -0.5
SLOT = 4096
BLK = 512
UC = 256
UNIT = 8 * UC
RAW = 3
PARTS = 2
BANK = 512

COLS = [(0, T_CTX), (T_CTX, T)]

EVENTS = 4 * (KC + 1)
EVENTS_FRONT = EVENTS - 7

C_ID, C_ROPE, C_IOTA = 0, P, P + 256
C_ALL = C_IOTA + ES

V_C, V_CTX, V_G1, V_G2, V_GA, V_GC, V_TAP = 0, 16, 32, 48, 64, 72, 80
V_ALL = V_TAP + 3 * CCH

MATS = [("g", 0), ("u", 0), ("g", 1), ("d", 0), ("u", 1), ("d", 1)]
PER_PAIR = 4 * len(MATS)
RING = 8
FIRST_BANKS = [1, 2, 5, 6]
LAST_BANKS = [2, 3, 0, 1]
ORDER = [4, 5, 6, 0, 2, 3, 7, 1]


def build(nc, x_prompt, x_sample, cache_k, cache_v, c, c_ctx, w_ada, b_ada, g_norm1, w_in, g_q, g_k, conv_w,
          g_attn_out, g_conv_out, w_out, g_norm2, w_router, w_gate, w_up, w_down, consts,
          y_prompt, y_sample, state_k, state_v):
    with ExitStack() as ctx:
        def sb(name, shape):
            return ctx.enter_context(nc.sbuf_tensor(name, shape, F32))

        def sem(name):
            return ctx.enter_context(nc.semaphore(name))

        def here():
            return -(-nc.sbuf_base // 32) * 32

        ring_at = here()
        ring = sb("ring", [P, RING, SLOT])
        res = sb("res", [P, KC * T])
        hid_at = here()
        hid = sb("hid", [P, KC * T])
        mix_at = here()
        mix = sb("mix", [P, KC * T])

        def parts_at(name, n, at):
            return nc.alloc_sbuf_tensor_at(name, [P, n], F32R, offset=at)

        raw = ring[:, 0:2, :].rearrange("p s n -> p (s n)")[:, 0:RAW * UNIT]
        w_parts = parts_at("w_parts", PARTS * 2 * UNIT, ring_at + 4 * RAW * UNIT)
        h_parts = parts_at("h_parts", 2 * KC * T, ring_at + 4 * 4 * SLOT)
        attn_parts = parts_at("attn_parts", 2 * AC * T, hid_at)
        conv_parts = parts_at("conv_parts", 2 * CCH * T, mix_at)
        hp = h_parts[:, :].rearrange("p (a k t) -> p a k t", a=2, t=T)
        ap = attn_parts[:, :].rearrange("p (a k t) -> p a k t", a=2, t=T)
        cp = conv_parts[:, :].rearrange("p (a k t) -> p a k t", a=2, t=T)

        def w_part(u, part):
            o = (u % PARTS * 2 + part) * UNIT
            return w_parts[:, o:o + UNIT]

        def raw_unit(u):
            return raw[:, u % RAW * UNIT:(u % RAW + 1) * UNIT]

        xT = res[:, :].rearrange("p (k t) -> p k t", k=KC)
        hT = hid[:, :].rearrange("p (k t) -> p k t", k=KC)
        mixT = mix[:, :].rearrange("p (k t) -> p k t", k=KC)
        x_rows = mix[:, :].rearrange("p (n d) -> p n d", n=NT)
        h2_rows = x_rows
        y_rows = x_rows
        xhatT = mixT
        q_rows = mix[:, AC * T:AC * T + NT * D_ATTN].rearrange("p (n d) -> p n d", n=NT)
        qT = mixT[:, 0:AC, :]

        at = [0]

        def piece(n):
            at[0] += n
            assert at[0] <= KC * T
            return hid[:, at[0] - n:at[0]]

        kv_flat = piece(NT * 2 * D_KV)
        kv_rows = kv_flat.rearrange("p (n d) -> p n d", n=NT)
        kT = piece(NKV * 512).rearrange("p (h t) -> p h t", h=NKV)
        kc = piece(D_KV)
        vc = piece(D_KV)
        assert at[0] == AC * T
        prob_flat = piece(2 * T)
        prob = prob_flat.rearrange("p (n t) -> p n t", n=2)
        vec_rows, bias_rows = prob_flat[0:V_ALL, 0:P], prob_flat[0:6 * KC, P:2 * P]
        probT_flat = piece(3 * T_LAT)
        probT = probT_flat.rearrange("p (j t) -> p j t", j=3)
        tmp = hid[:, at[0] - 2 * T - 3 * T_LAT:at[0]]
        gqk = piece(2 * HD)
        at[0] = cu_at = KC * T - 3 * T
        cu_flat = piece(2 * T)
        cu = cu_flat.rearrange("p (j t) -> p j t", j=2)
        cv = piece(T)
        LO_EARLY = (cu_at - AC * T) // T
        sq1 = [probT_flat[:, 0:T], probT_flat[:, T:2 * T]]
        ssum1 = cu_flat[:, 0:T]
        late = ring[:, 3, SLOT // 2:]
        sq = [late[:, 0:T], late[:, T:2 * T]]
        ssum = [late[:, 2 * T:3 * T], late[:, 3 * T:4 * T]]
        mod_rows = [late[:, 4 * T:4 * T + BANK], kv_flat[:, 0:BANK]]
        ada_buf = [ring[:, 7, 0:D], ring[:, 7, D:2 * D]]
        sq2, ssum2 = sq, ssum[0]
        rt = ring[:, 1, :]
        rstd2 = rt[:, 0:T]
        affT, work, mask, rank = (rt[0:NE, n * T:(n + 1) * T] for n in (1, 2, 3, 4))
        lg = rt[:, 5 * T:5 * T + NT * NE].rearrange("p (n e) -> p n e", n=NT)
        r_small = rt[:, 5 * T + 64:5 * T + 64 + 16]
        lg_parts = rt[:, 6 * T:7 * T]
        top8 = rt[0:NE, 5 * T + 96:5 * T + 96 + 8]

        ident = sb("ident", [P, P])
        iota = sb("iota", [P, ES])
        early = sb("early", [P, 32 * KC + KC * NE + P + 256])
        cond = early[:, 0:32 * KC].rearrange("p (k n) -> p k n", k=KC)
        wr = early[:, 32 * KC:32 * KC + KC * NE].rearrange("p (k e) -> p k e", k=KC)
        ones = early[:, 32 * KC + KC * NE:32 * KC + KC * NE + P]
        rope = early[:, 32 * KC + KC * NE + P:]
        give = early[:, 0:9 * ES].rearrange("p (t s) -> p t s", t=NT)
        pick = early[:, 9 * ES:15 * ES]
        vecT = sb("vecT", [P, V_ALL])
        biasT = sb("biasT", [P, N_MOD * KC])
        mod3 = sb("mod", [P, N_MOD * KC, 2])
        gain = sb("gain", [P, 2, KC, 2])
        stat = sb("stat", [P, 32])
        slotP = sb("slotP", [P, 6 * PAIRS])
        affP = sb("affP", [P, 6 * PAIRS])

        moe_at = [0]

        def moe_piece(n):
            moe_at[0] += n
            assert moe_at[0] <= KC * T
            return hid[:, moe_at[0] - n:moe_at[0]]

        xs = moe_piece(KC * PW).rearrange("p (k s) -> p k s", k=KC)
        act = moe_piece(BANK)
        actT = moe_piece(BANK)
        y_sb = [moe_piece(2 * BANK), moe_piece(2 * BANK)]
        giveT = [moe_piece(T), moe_piece(T)]

        psum = ctx.enter_context(nc.psum_tensor("psum", [P, 8, BANK], F32))
        bank = [psum[:, i, :] for i in range(8)]

        small_in, cache_in, wr_in = sem("small_in"), sem("cache_in"), sem("wr_in")
        x_in = [sem(f"x_in{n}") for n in range(NT)]
        w_landed = [sem(f"w_landed{n}") for n in range(4)]
        w_used = sem("w_used")
        raw_landed = [sem(f"raw_landed{n}") for n in range(RAW)]
        hi_ready, lo_ready, unit_used = sem("hi_ready"), sem("lo_ready"), sem("unit_used")
        h_hi, h_parts_ready = sem("h_hi"), sem("h_parts_ready")
        normed, mix_hi = sem("normed"), sem("mix_hi")
        ada_landed = [sem("ada_landed0"), sem("ada_landed1")]
        ada_free = sem("ada_free")
        moe_landed = [sem(f"moe_landed{n}") for n in range(RING)]
        moe_used = sem("moe_used")
        vec_turned, vec_ready, cond_ready = sem("vec_turned"), sem("vec_ready"), sem("cond_ready")
        x_turned, x_out_dve, x_out_act = sem("x_turned"), sem("x_out_dve"), sem("x_out_act")
        sq_ready, sq_added, sums_done = sem("sq_ready"), sem("sq_added"), sem("sums_done")
        var_ready, std_ready = sem("var_ready"), sem("std_ready")
        gains_ready, mod_rows_out, mod_turned, mod_read = sem("gains_ready"), sem("mod_rows_out"), sem("mod_turned"), sem("mod_read")
        h_dve, h_act = sem("h_dve"), sem("h_act")
        qkv_acc, qkv_out = sem("qkv_acc"), sem("qkv_out")
        conv_acc, conv_out = sem("conv_acc"), sem("conv_out")
        qk_ready, qk_turned, qkT_ready = sem("qk_ready"), sem("qk_turned"), sem("qkT_ready")
        score_done, max_ready, exp_done, prob_ready = sem("score_done"), sem("max_ready"), sem("exp_done"), sem("prob_ready")
        prob_turned, probT_ready, o_done, o_out = sem("prob_turned"), sem("probT_ready"), sem("o_done"), sem("o_out")
        osq_ready, osq_added = sem("osq_ready"), sem("osq_added")
        csq_ready, csq_added = sem("csq_ready"), sem("csq_added")
        mix_ready = sem("mix_ready")
        out_acc, x1_ready = sem("out_acc"), sem("x1_ready")
        sq2_ready, sq2_added = sem("sq2_ready"), sem("sq2_added")
        h2n_ready, h2_act, h2_dve = sem("h2n_ready"), sem("h2_act"), sem("h2_dve")
        logits_done, logits_out, logits_turned, shifted, exp2_done, aff_ready = sem("logits_done"), sem("logits_out"), sem("logits_turned"), sem("shifted"), sem("exp2_done"), sem("aff_ready")
        aff_turned, rank_ready, rank_turned, routed = sem("aff_turned"), sem("rank_ready"), sem("rank_turned"), sem("routed")
        rows_turned, rows_out = sem("rows_turned"), sem("rows_out")
        pick_ready, gathered, xs_dve, xs_act = sem("pick_ready"), sem("gathered"), sem("xs_dve"), sem("xs_act")
        give_ready, give_turned, giveT_ready = sem("give_ready"), sem("give_turned"), sem("giveT_ready")
        sil_ready, act_ready, act_turned, actT_ready = sem("sil_ready"), sem("act_ready"), sem("act_turned"), sem("actT_ready")
        y_out, y_last, sent, added = sem("y_out"), sem("y_last"), sem("sent"), sem("added")
        last_turned, last_out = sem("last_turned"), sem("last_out")
        dve_chain = sem("dve_chain")
        state_out, y_stored = sem("state_out"), sem("y_stored")

        ada_rows = w_ada[0]
        in_rows = w_in[0].rearrange("(k p) n -> p k n", p=P)
        out_rows = w_out[0].rearrange("(k p) n -> p k n", p=P)
        gate_rows = w_gate.rearrange("a e d f -> (a e d) f")
        up_rows = w_up.rearrange("a e d f -> (a e d) f")
        down_rows = w_down.rearrange("a e f d -> (a e f) d")

        o_b = D_ATTN + 2 * D_KV
        o_c, o_u = o_b + D_CONV, o_b + 2 * D_CONV
        N_ADA1 = KC
        U_QKV = 2 * o_b // UC
        U_CONV = 2 * 3 * D_CONV // UC
        U_OUT = 2 * D // UC
        U_ALL = U_QKV + U_CONV + U_OUT
        OUT_UNITS = [(0, 0), (1, 0), (0, 1), (1, 1)] + [(b, half) for b in range(2, U_OUT // 2) for half in range(2)]

        DRAINED = [[], [], [0], [1, 2], [3]] + [[s - 1] for s in range(5, U_OUT + 1)]

        def chunks_of(q):
            return range(4 * q, 4 * q + 4)

        class Chain:

            def __init__(self, eng, s):
                self.eng, self.s, self.n = eng, s, 0

            def link(self, ins):
                self.n += 1
                ins.then_inc(self.s, 1)
                self.eng.wait_ge(self.s, self.n)

        block = ctx.enter_context(nc.Block())

        @block.sync
        def _(sp):
            for n in range(NT):
                src = x_prompt[0] if n == 0 else x_sample[0, (n - 1) * P:n * P, :]
                sp.dma_start(x_rows[:, n, :], src).then_inc(x_in[n], 16)

            sp.wait_ge(small_in, 16 * 11)
            for n in range(4):
                sp.dma_start(ring[:, n, :], ada_rows[n * P:(n + 1) * P, 0:SLOT]).then_inc(w_landed[n], 16)
            with sp.Fori(1, N_ADA1 // 4) as i:
                for n in range(4):
                    sp.wait_ge(w_used, 4 * i + (n - 3))
                    sp.dma_start(ring[:, n, :], ada_rows[bass.ds(i * 4 * P + n * P, P), 0:SLOT]).then_inc(w_landed[n], 16)

            def unit_load(u, src, half, col, more=0):
                if u >= RAW:
                    sp.wait_ge(lo_ready, more + (u - RAW + 1))
                elif u == RAW - 1:
                    sp.wait_ge(w_used, N_ADA1 - 2)
                elif u == 0:
                    sp.wait_ge(w_used, N_ADA1 - 3)
                sp.dma_start(raw_unit(u).rearrange("p (k n) -> p k n", n=UC), src[:, 8 * half:8 * half + 8, bass.ds(col, UC)])\
                    .then_inc(raw_landed[u % RAW], 16)

            for u in range(U_QKV):
                unit_load(u, in_rows, u % 2, u // 2 * UC)
            with sp.Fori(0, D_CONV // UC) as i:
                for j in range(6):
                    unit_load(U_QKV + j, in_rows, j % 2, i * UC + (o_u, o_c, o_b)[j // 2], 6 * i)
            for j, (b, half) in enumerate(OUT_UNITS):
                unit_load(U_QKV + U_CONV + j, out_rows, half, b * UC)

            def expert_load(pair, q):
                what, e = MATS[q // 4]
                part, slot = q % 4, ORDER[q % RING]
                dst = ring[:, slot, :]
                if what == "d":
                    src = down_rows[bass.ds(pair * 2 * FF + e * FF, FF), part * BLK:(part + 1) * BLK].rearrange("(k p) n -> p k n", p=P)
                    dst = dst.rearrange("p (k n) -> p k n", n=BLK)
                else:
                    src = (gate_rows if what == "g" else up_rows)[bass.ds(pair * 2 * D + e * D + part * 512, 512), :]\
                        .rearrange("(k p) n -> p k n", p=P)
                    dst = dst.rearrange("p (k n) -> p k n", k=4)
                sp.dma_start(dst, src).then_inc(moe_landed[slot], 16)

            sp.wait_ge(unit_used, U_QKV + U_CONV)
            for q in range(RING):
                if ORDER[q] == 7:
                    sp.wait_ge(ada_free, 2 + 64)
                if ORDER[q] == 0:
                    sp.wait_ge(lo_ready, U_ALL)
                if ORDER[q] == 2:
                    sp.wait_ge(unit_used, U_ALL)
                if ORDER[q] == 3:
                    sp.wait_ge(sums_done, 4)
                if ORDER[q] == 1:
                    sp.wait_ge(routed, 1)
                expert_load(0, q)
            with sp.Fori(0, PAIRS - 1) as i:
                for j in range(PER_PAIR):
                    sp.wait_ge(moe_used, PER_PAIR * i + (j + 1))
                    expert_load(i + (j + RING) // PER_PAIR, (j + RING) % PER_PAIR)
            for j in range(PER_PAIR - RING):
                sp.wait_ge(moe_used, PER_PAIR * (PAIRS - 1) + j + 1)
                expert_load(PAIRS - 1, j + RING)

            for q in range(4):
                cols = slice(q * BLK, (q + 1) * BLK)
                sp.wait_ge(last_out, NT * (q + 1))
                sp.dma_start(y_prompt[0, :, cols], y_rows[:, 0, cols]).then_inc(y_stored, 16)
                sp.dma_start(y_sample[0, :, cols].rearrange("(n p) d -> p n d", p=P), y_rows[:, 1:NT, cols]).then_inc(y_stored, 16)
            sp.wait_ge(y_stored, 16 * 8)

        @block.gpsimd
        def _(pool):
            nc.gpsimd.memset(ones, 1.0).then_inc(ada_free, 1)
            nc.gpsimd.memset(cond, 0.0).then_inc(ada_free, 1)
            for m in range(2, N_MOD):
                with pool.Fori(0, KC // 2) as i:
                    for j in range(2):
                        pool.wait_ge(ada_free, 2 * i + (KC * (m - 2) + j + 1))
                        pool.dma_start(ada_buf[j], ada_rows[bass.ds(i * 2 * P + j * P, P), m * D:(m + 1) * D])\
                            .then_inc(ada_landed[j], 16)

        @block.tensor
        def _(pe):
            def mm(out, lhsT, rhs, start, stop):
                return nc.tensor.matmul(out, lhsT, rhs, start=start, stop=stop, skip_group_check=True)

            pe.wait_ge(small_in, 16 * 11)
            nc.tensor.transpose(bank[1][:, 0:V_ALL], vec_rows, ident[0:V_ALL, 0:V_ALL])
            nc.tensor.transpose(bank[2][:, 0:N_MOD * KC], bias_rows, ident[0:N_MOD * KC, 0:N_MOD * KC]).then_inc(vec_turned, 1)

            def turn_groups(groups, src, banks, done, free):
                for g in groups:
                    free(g)
                    for j in range(4):
                        last = nc.tensor.transpose(banks[g % len(banks)][:, j * P:(j + 1) * P], src(g, j), ident[:, :])
                    last.then_inc(done, 1)

            def x_free(g):
                if g % 4 == 0:
                    pe.wait_ge(x_in[g // 4], 16)
                if g >= 4:
                    pe.wait_ge(x_out_act if g % 2 else x_out_dve, (g - 4) // 2 + 1)
            turn_groups(range(12), lambda g, j: x_rows[:, g // 4, (g % 4 * 4 + j) * P:(g % 4 * 4 + j + 1) * P],
                        bank[4:8], x_turned, x_free)
            def ada(out, k, weights, first):
                for j in range(4):
                    last = mm(out[32 * j:32 * j + 32, :], cond[:, k, :], weights[:, j * BLK:(j + 1) * BLK], first, k == KC - 1)
                return last

            def turn_mod(out, rows):
                for j in range(4):
                    last = nc.tensor.transpose(out[:, j * P:(j + 1) * P], rows[:, j * P:(j + 1) * P], ident[:, :])
                last.then_inc(mod_turned, 1)

            pe.wait_ge(cond_ready, 1)
            for k in range(N_ADA1):
                pe.wait_ge(w_landed[k % 4], 16 * (k // 4 + 1))
                for m in range(2):
                    last = ada(bank[m], k, ring[:, k % 4, m * D:(m + 1) * D], k == 0)
                last.then_inc(w_used, 1)
                if k == 4:
                    pe.wait_ge(ada_free, 2)
                    pe.wait_ge(sq_added, KC)
                    mm(bank[3][:, 0:T], ones, ssum1, True, True).then_inc(sums_done, 1)
            for m in range(2):
                pe.wait_ge(mod_rows_out, m + 1)
                turn_mod(bank[2 + m], mod_rows[m])

            def event(n):
                m, k = 2 + n // (KC + 1), n % (KC + 1)
                if k < KC:
                    t = KC * (m - 2) + k
                    if k == 0 and m > 2:
                        pe.wait_ge(mod_read, m)
                    pe.wait_ge(ada_landed[t % 2], 16 * (t // 2 + 1))
                    ada(bank[0], k, ada_buf[t % 2], k == 0).then_inc(ada_free, 1)
                else:
                    pe.wait_ge(mod_rows_out, m + 1)
                    turn_mod(bank[0], mod_rows[0])

            THREE = ((0, 0), (0, 1), (1, 0))

            def weights_tile(u, kk, j, part):
                return w_part(u, part)[:, kk * UC + j * P:kk * UC + (j + 1) * P]

            events = 0
            for u in range(U_QKV):
                b, half = u // 2, u % 2
                pe.wait_ge(lo_ready, u + 1)
                for kk in range(8):
                    k = 8 * half + kk
                    if b == 0:
                        pe.wait_ge(h_parts_ready, k + 1)
                    for t in range(NT):
                        if k == 0 and b >= 2:
                            pe.wait_ge(qkv_out, NT * (b - 2) + t + 1)
                        for wp, hh in THREE:
                            last = mm(bank[1 + NT * (b % 2) + t][:, 0:UC], hp[:, hh, k, t * P:(t + 1) * P],
                                      w_part(u, wp)[:, kk * UC:(kk + 1) * UC], k == 0 and wp + hh == 0, k == KC - 1 and wp == 1)
                        if k == KC - 1 and t < NT - 1:
                            last.then_inc(qkv_acc, 1)
                    if kk == 7:
                        last.then_inc(unit_used, 1)
                    if kk in (2, 6):
                        event(events)
                        events += 1

            def turn_qk(t):
                pe.wait_ge(qk_ready, 5)
                if t:
                    pe.wait_ge(qkT_ready, t)
                else:
                    pe.wait_ge(qkv_out, NT * U_QKV // 2)
                for h in range(NH):
                    nc.tensor.transpose(bank[5 + h // 4][:, (h % 4) * P:(h % 4 + 1) * P],
                                        q_rows[:, t, h * HD:(h + 1) * HD], ident[:, :])
                if t == 0:
                    pe.wait_ge(cache_in, 64)
                    for h in range(NKV):
                        nc.tensor.transpose(bank[7][:, (2 + h) * P:(3 + h) * P], kc[:, h * HD:(h + 1) * HD], ident[:, :])
                for h in range(NKV):
                    last = nc.tensor.transpose(bank[7][:, h * P:(h + 1) * P], kv_rows[:, t, h * HD:(h + 1) * HD], ident[:, :])
                last.then_inc(qk_turned, 1)

            def unit(n):
                h = n % NH
                kv = h // GROUP
                v = [kv_rows[:, t, D_KV + kv * HD:D_KV + (kv + 1) * HD] for t in range(NT)]
                if n < NH:
                    return h, [0], kT[:, kv, 0:P], v[0:1]
                return h, [1, 2], kT[:, kv, P:4 * P], [vc[:, kv * HD:(kv + 1) * HD]] + v[1:]

            def scores(n):
                h, tiles, keys, v = unit(n)
                pe.wait_ge(qkT_ready, NT)
                if n:
                    pe.wait_ge(exp_done, n)
                for i, t in enumerate(tiles):
                    last = mm(bank[3 + i][:, 0:len(v) * P], qT[:, h, t * P:(t + 1) * P], keys, True, True)
                last.then_inc(score_done, 1)

            def turn_prob(n):
                h, tiles, keys, v = unit(n)
                pe.wait_ge(prob_ready, n + 1)
                if n:
                    pe.wait_ge(probT_ready, n)
                for j in range(len(v)):
                    for i in range(len(tiles)):
                        last = nc.tensor.transpose(bank[5 + j // 2][:, (2 * (j % 2) + i) * P:(2 * (j % 2) + i + 1) * P],
                                                   prob[:, i, j * P:(j + 1) * P], ident[:, :])
                last.then_inc(prob_turned, 1)

            def values(n):
                h, tiles, keys, v = unit(n)
                w = len(tiles) * P
                pe.wait_ge(probT_ready, n + 1)
                if n:
                    pe.wait_ge(o_out, n)
                for j, vj in enumerate(v):
                    last = mm(bank[7][:, 0:w], vj, probT[:, j, 0:w], j == 0, j == len(v) - 1)
                last.then_inc(o_done, 1)

            def half_chunk(u, j, half, values, ready=None, out=None):
                out = out or 1 + j
                for kk in range(8):
                    k = 8 * half + kk
                    if ready:
                        pe.wait_ge(ready, k + 1)
                    for wp, hh in THREE:
                        last = mm(bank[out][:, 0:T], weights_tile(u, kk, j, wp), values(hh, k),
                                  k == 0 and wp + hh == 0, k == KC - 1 and wp == 1)
                return last

            for s in range(U_CONV):
                u, g = U_QKV + s, s // 2 * 2
                pe.wait_ge(lo_ready, u + 1)
                for j in range(2):
                    if s == 0:
                        pe.wait_ge(qkv_out, NT * 4 + j + 1)
                    elif s % 2 == 0:
                        pe.wait_ge(conv_out, g + j - 1)
                    last = half_chunk(u, j, s % 2, lambda hh, k: hp[:, hh, k, :])
                    if j == 1:
                        last.then_inc(unit_used, 1)
                    elif s % 2:
                        last.then_inc(conv_acc, 1)
                    if events < EVENTS_FRONT:
                        event(events)
                        events += 1
                if s < NT:
                    turn_qk(s)
                if 0 <= s - 3 < 2 * NH:
                    scores(s - 3)
                if 0 <= s - 4 < 2 * NH:
                    turn_prob(s - 4)
                if 0 <= s - 5 < 2 * NH:
                    values(s - 5)
                if s == 21:
                    pe.wait_ge(osq_added, 2 * NH)
                    mm(bank[3][:, 0:T], ones, ssum[0], True, True).then_inc(sums_done, 1)

            def mixed(hh, k):
                return ap[:, hh, k, :] if k < AC else cp[:, hh, k - AC, :]

            for n in range(4):
                b, half = OUT_UNITS[n]
                u = U_QKV + U_CONV + n
                pe.wait_ge(lo_ready, u + 1)
                for j in range(2):
                    if n == 0:
                        pe.wait_ge(conv_out, 23 + j)
                    last = half_chunk(u, j, half, mixed, mix_ready if b == 0 and j == 0 else None, FIRST_BANKS[2 * b + j])
                    if j == 1:
                        last.then_inc(unit_used, 1)
                    elif half:
                        last.then_inc(out_acc, 1)
                    if n == 0 and j == 0:
                        pe.wait_ge(csq_added, CCH)
                        mm(bank[4][:, 0:T], ones, ssum[1], True, True).then_inc(sums_done, 1)

            def out_block(b, more):
                for half in range(2):
                    u = U_QKV + U_CONV + 2 * b + half
                    pe.wait_ge(lo_ready, 2 * more + (u + 1))
                    for j in range(2):
                        if half == 0:
                            pe.wait_ge(x1_ready, 2 * more + (2 * b + j - 1))
                        last = half_chunk(u, j, half, mixed)
                        if j == 1:
                            last.then_inc(unit_used, 1)
                        elif half:
                            last.then_inc(out_acc, 1)

            with pe.Fori(0, 3) as i:
                out_block(2, 2 * i)
                out_block(3, 2 * i)
            pe.wait_ge(sq2_added, KC - 2)
            mm(bank[3][:, 0:T], ones, ssum2, True, False)
            pe.wait_ge(sq2_ready, KC - 1)
            mm(bank[3][:, 0:T], ones, sq2[0], False, False)
            pe.wait_ge(sq2_ready, KC)
            mm(bank[3][:, 0:T], ones, sq2[1], False, True).then_inc(sums_done, 1)
            event(EVENTS_FRONT)
            event(EVENTS_FRONT + 1)

            pe.wait_ge(wr_in, 16)
            for k in range(KC):
                if k % 3 < 2:
                    pe.wait_ge(h2_act, k - k // 3 + 1)
                else:
                    pe.wait_ge(h2_dve, k // 3 + 1)
                j = 32 * (k % 4)
                last = mm(bank[4][j:j + NE, 0:T], wr[:, k, :], hT[:, k, :], k < 4, k >= KC - 4)
            last.then_inc(logits_done, 1)
            event(EVENTS_FRONT + 2)
            event(EVENTS_FRONT + 3)

            def rows_free(g):
                if g >= 4:
                    pe.wait_ge(rows_out, g - 3)

            def rows_src(g, j):
                return hT[:, g % 4 * 4 + j, g // 4 * P:(g // 4 + 1) * P]
            rows_banks = [bank[5], bank[6], bank[7], bank[1]]
            turn_groups(range(1), rows_src, rows_banks, rows_turned, rows_free)
            pe.wait_ge(logits_out, 1)
            for t in range(NT):
                last = nc.tensor.transpose(bank[3][:, t * P:(t + 1) * P], lg_parts[:, t * P:(t + 1) * P], ident[:, :])
            last.then_inc(logits_turned, 1)
            turn_groups(range(1, 8), rows_src, rows_banks, rows_turned, rows_free)
            pe.wait_ge(aff_ready, 1)
            for t in range(NT):
                last = nc.tensor.transpose(bank[3][0:NE, t * P:(t + 1) * P], lg[:, t, :], ident[:, :])
            last.then_inc(aff_turned, 1)
            turn_groups(range(8, 12), rows_src, rows_banks, rows_turned, rows_free)
            event(EVENTS_FRONT + 4)
            event(EVENTS_FRONT + 5)
            pe.wait_ge(rank_ready, 1)
            for t in range(NT):
                last = nc.tensor.transpose(bank[4][:, t * NE:(t + 1) * NE], rank[:, t * P:(t + 1) * P], ident[0:NE, 0:NE])
            last.then_inc(rank_turned, 1)

            def gather_quarter(q):
                for kk in range(4):
                    k = 4 * q + kk
                    for t in range(NT):
                        last = mm(bank[4 + q][:, kk * PW:(kk + 1) * PW], h2_rows[:, t, k * P:(k + 1) * P],
                                  pick[:, t * PW:(t + 1) * PW], t == 0, t == NT - 1)
                last.then_inc(gathered, 1)

            def gather(i):
                pe.wait_ge(pick_ready, i + 1)
                for q in range(4):
                    gather_quarter(q)

            def send_chunk(k, b):
                n, o = k // 2 % 2, k // 4 * UC + k % 2 * P
                mm(bank[b][:, 0:T], y_sb[n][:, o:o + P], giveT[n], True, True).then_inc(sent, 1)

            def up_or_gate(slot, what, e, part):
                for kk in range(4):
                    k = 4 * part + kk
                    for half in range(2):
                        off = kk * FF + half * BLK
                        last = mm(bank[0 if what == "g" else 1][ES * half:ES * half + ES, :],
                                  xs[:, k, e * ES:(e + 1) * ES], ring[:, slot, off:off + BLK], k == 0, k == KC - 1)
                return last

            def down(slot, e, part, out):
                for f in range(FC):
                    rows = actT[:, (f % 4) * P + (f // 4) * ES:(f % 4) * P + (f // 4 + 1) * ES]
                    for half in range(2):
                        off = (2 * f + half) * UC
                        row = ES * (half ^ e)
                        last = mm(out[row:row + ES, :], rows, ring[:, slot, off:off + UC], f == 0, f == FC - 1)
                return last

            def turn_act(i, e):
                pe.wait_ge(act_ready, 2 * i + (e + 1))
                for j in range(4):
                    last = nc.tensor.transpose(bank[4][:, j * P:(j + 1) * P], act[:, j * P:(j + 1) * P], ident[:, :])
                last.then_inc(act_turned, 1)
                pe.wait_ge(giveT_ready, 2 * i + 2)
                pe.wait_ge(actT_ready, 2 * i + (e + 1))

            def landed(i, q):
                pe.wait_ge(moe_landed[ORDER[q % RING]], 48 * i + 16 * (q // RING + 1))

            def round_of(i, first=False, last_pair=False):
                for q in range(PER_PAIR):
                    what, e = MATS[q // 4]
                    part, slot = q % 4, ORDER[q % RING]
                    start = first and e == 0
                    if part == 0 and what == "g":
                        if e == 0 and not first:
                            pe.wait_ge(xs_dve, 2 * i + 2)
                            pe.wait_ge(xs_act, 2 * i + 2)
                        if not start:
                            pe.wait_ge(sil_ready, 2 * i + e)
                    if first and q < 4:
                        for quarter in ([0, 1], [2], [3], [])[q]:
                            gather_quarter(quarter)
                        if q == 0:
                            pe.wait_ge(mod_rows_out, N_MOD)
                            turn_mod(bank[2], act)
                        pe.wait_ge(xs_dve if q % 2 else xs_act, q // 2 + 1)
                    if part == 0 and what == "u" and not start:
                        pe.wait_ge(act_ready, 2 * i + e)
                    if part == 0 and what == "d":
                        if e == 1 and not last_pair:
                            gather(i + 1)
                            pe.wait_ge(xs_act, 2 * i + 3)
                        if not first:
                            pe.wait_ge(added, 16 * i)
                        if not start:
                            pe.wait_ge(y_out, 2 * i + e)
                        turn_act(i, e)
                    landed(i, q)
                    if what != "d":
                        last = up_or_gate(slot, what, e, part)
                    elif last_pair and e == 1:
                        last = down(slot, e, part, bank[LAST_BANKS[part]][:, 0:UC])
                    else:
                        last = down(slot, e, part, bank[2 + part // 2][:, part % 2 * UC:(part % 2 + 1) * UC])
                    last.then_inc(moe_used, 1)
                    if q == 7:
                        if not first:
                            pe.wait_ge(y_out, 2 * i)
                        else:
                            pe.wait_ge(mod_read, N_MOD)
                        if not first:
                            for k in range(KC):
                                if k >= 4:
                                    pe.wait_ge(added, 16 * i + (k - 19))
                                send_chunk(k, 4 + k % 4)
                        pe.wait_ge(give_ready, i + 1)
                        for n in range(2):
                            for t in range(NT):
                                last = nc.tensor.transpose(bank[2 + n][:, t * P:(t + 1) * P], give[:, t, n * ES:n * ES + P], ident[:, :])
                            last.then_inc(give_turned, 1)
                    if last_pair and q >= PER_PAIR - 4:
                        if part:
                            turn_result(part - 1)
                        send_last(part)

            def send_last(q):
                pe.wait_ge(y_last, q + 1)
                if q == 0:
                    pe.wait_ge(y_out, 2 * PAIRS - 1)
                for k, b in zip(chunks_of(q), [4, 5, 6, 7] if q == 0 else [7, 4, 5, 6]):
                    if q and b < 7:
                        pe.wait_ge(last_out, NT * (q - 1) + b - 3)
                    send_chunk(k, b)

            def turn_result(q):
                pe.wait_ge(added, 16 * (PAIRS - 1) + 4 * (q + 1))
                for t in range(NT):
                    for j, k in enumerate(chunks_of(q)):
                        last = nc.tensor.transpose(bank[4 + t][:, j * P:(j + 1) * P], xT[:, k, t * P:(t + 1) * P], ident[:, :])
                    last.then_inc(last_turned, 1)

            pe.wait_ge(rows_out, 12)
            pe.wait_ge(pick_ready, 1)
            round_of(0, first=True)
            with pe.Fori(1, PAIRS - 1) as i:
                round_of(i)
            round_of(PAIRS - 1, last_pair=True)
            turn_result(3)

        @block.scalar
        def _(act_e):
            a = act_e

            def copy(out, in_):
                return nc.scalar.activation(out, in_, ACT.Copy)

            a.dma_start(ident[:, :], consts[:, C_ID:C_ID + P]).then_inc(small_in, 16)
            a.dma_start(rope, consts[:, C_ROPE:C_ROPE + 256]).then_inc(small_in, 16)
            a.dma_start(iota[:, :], consts[:, C_IOTA:C_IOTA + ES]).then_inc(small_in, 16)
            for src, row, n in ((c, V_C, 16), (c_ctx.rearrange("(a d) -> a d", a=1), V_CTX, 16), (g_norm1, V_G1, 16),
                                (g_norm2, V_G2, 16), (g_attn_out, V_GA, AC), (g_conv_out, V_GC, CCH)):
                a.dma_start(vec_rows[row:row + n, :], src[0].rearrange("(k p) -> k p", p=P)).then_inc(small_in, 16)
            a.dma_start(vec_rows[V_TAP:V_ALL, :], conv_w[0].rearrange("w (k p) -> (w k) p", p=P)).then_inc(small_in, 16)
            a.dma_start(bias_rows, b_ada[0].rearrange("(k p) -> k p", p=P)).then_inc(small_in, 16)

            a.wait_ge(vec_ready, 1)
            a.wait_ge(ada_free, 2)
            nc.scalar.activation(cond[:, :, 0], vecT[:, V_CTX:V_CTX + KC], ACT.Silu)
            nc.scalar.activation(cond[:, :, 1], vecT[:, V_C:V_C + KC], ACT.Silu).then_inc(cond_ready, 1)

            for g in range(1, 12, 2):
                a.wait_ge(x_turned, g + 1)
                t, kk = g // 4, g % 4 * 4
                copy(xT[:, kk:kk + 4, t * P:(t + 1) * P], bank[4 + g % 4][:, :].rearrange("p (j t) -> p j t", j=4))\
                    .then_inc(x_out_act, 1)
            a.wait_ge(x_out_act, 6)
            a.wait_ge(x_out_dve, 6)
            for k in range(KC):
                if k >= 2:
                    a.wait_ge(sq_added, k - 1)
                nc.scalar.activation(sq1[k % 2], xT[:, k, :], ACT.Square).then_inc(sq_ready, 1)

            roots = [0]

            def root(ap):
                roots[0] += 1
                a.wait_ge(var_ready, roots[0])
                nc.scalar.activation(ap, ap, ACT.Sqrt).then_inc(std_ready, 1)

            root(ssum1)

            def hi_part(u):
                if u >= PARTS:
                    a.wait_ge(unit_used, u - PARTS + 1)
                a.wait_ge(raw_landed[u % RAW], 16 * (u // RAW + 1))
                copy(w_part(u, 0), raw_unit(u)).then_inc(hi_ready, 1)

            a.wait_ge(w_used, N_ADA1 - 1)
            hi_part(0)
            a.wait_ge(gains_ready, 1)
            for k in range(1, KC, 2):
                for n, (lo, hi) in enumerate(COLS):
                    last = nc.scalar.activation(xhatT[:, k, lo:hi], xhatT[:, k, lo:hi], ACT.Identity,
                                                scale=gain[:, 0, k, n:n + 1], bias=mod3[:, k, n:n + 1])
                last.then_inc(h_act, 1)
                a.wait_ge(h_dve, k // 2 + 1)
                copy(hp[:, 0, k - 1, :], xhatT[:, k - 1, :]).then_inc(h_hi, 1)
                a.wait_ge(h_act, k // 2 + 1)
                copy(hp[:, 0, k, :], xhatT[:, k, :]).then_inc(h_hi, 1)
                if k == 7:
                    hi_part(1)

            a.dma_start(kc, cache_k[0, 0].rearrange("s h d -> s (h d)")).then_inc(cache_in, 16)
            a.dma_start(vc, cache_v[0, 0].rearrange("s h d -> s (h d)")).then_inc(cache_in, 16)
            a.dma_start(gqk[:, 0:HD], g_q[0].partition_broadcast(P)).then_inc(cache_in, 16)
            a.dma_start(gqk[:, HD:2 * HD], g_k[0].partition_broadcast(P)).then_inc(cache_in, 16)
            a.dma_start(wr, w_router[0].rearrange("(k p) e -> p k e", p=P)).then_inc(wr_in, 16)

            for u in range(U_QKV):
                if u:
                    hi_part(u + 1)
                if u and u % 2 == 0:
                    root(stat[:, 0:2 * NT])
                if u % 2:
                    b = u // 2
                    for t in range(NT):
                        if t < NT - 1:
                            a.wait_ge(qkv_acc, (NT - 1) * b + t + 1)
                        else:
                            a.wait_ge(unit_used, u + 1)
                        dst = kv_rows[:, t, (b - 4) * UC:(b - 3) * UC] if b >= 4 else q_rows[:, t, b * UC:(b + 1) * UC]
                        copy(dst, bank[1 + NT * (b % 2) + t][:, 0:UC]).then_inc(qkv_out, 1)

            def csq(m):
                a.wait_ge(conv_out, m // 2 * 6 + m % 2 + 5)
                if m:
                    a.wait_ge(csq_added, m)
                nc.scalar.activation(sq[1], mixT[:, AC + m, :], ACT.Square).then_inc(csq_ready, 1)

            for s in range(U_CONV + 1):
                hi_part(U_QKV + s + 1)
                if s == 0:
                    a.wait_ge(qk_ready, 5)
                    a.wait_ge(qkv_out, NT * U_QKV // 2)
                    a.dma_start(state_k[0, 0].rearrange("s h d -> s (h d)"), kv_rows[:, 0, 0:D_KV]).then_inc(state_out, 16)
                    a.dma_start(state_v[0, 0].rearrange("s h d -> s (h d)"), kv_rows[:, 0, D_KV:2 * D_KV]).then_inc(state_out, 16)
                if 0 <= s - 1 < NT:
                    t = s - 1
                    a.wait_ge(qk_turned, t + 1)
                    copy(qT[:, 0:4, t * P:(t + 1) * P], bank[5][:, :].rearrange("p (h t) -> p h t", h=4))
                    copy(qT[:, 4:8, t * P:(t + 1) * P], bank[6][:, :].rearrange("p (h t) -> p h t", h=4))
                    if t == 0:
                        copy(kT[:, :, P:2 * P], bank[7][:, 2 * P:4 * P].rearrange("p (h t) -> p h t", h=2))
                    at_col = 0 if t == 0 else (1 + t) * P
                    copy(kT[:, :, at_col:at_col + P], bank[7][:, 0:2 * P].rearrange("p (h t) -> p h t", h=2))\
                        .then_inc(qkT_ready, 1)
                n = s - 4
                if 0 <= n < 2 * NH:
                    tiles, nk = (1, 1) if n < NH else (2, 3)
                    a.wait_ge(max_ready, n + 1)
                    if n:
                        a.wait_ge(prob_turned, n)
                    for i in range(tiles):
                        last = nc.scalar.activation(prob[:, i, 0:nk * P], bank[3 + i][:, 0:nk * P], ACT.Exp,
                                                    scale=SCALE, bias=stat[:, 12 + i:13 + i], accum_out=stat[:, 14 + i:15 + i])
                    last.then_inc(exp_done, 1)
                n = s - 5
                if 0 <= n < 2 * NH:
                    a.wait_ge(prob_turned, n + 1)
                    if n:
                        a.wait_ge(o_done, n)
                    if n < NH:
                        last = copy(probT[:, 0, 0:P], bank[5][:, 0:P])
                    else:
                        copy(probT[:, 0:2, :], bank[5][:, :].rearrange("p (j t) -> p j t", j=2))
                        last = copy(probT[:, 2, :], bank[6][:, 0:T_LAT])
                    last.then_inc(probT_ready, 1)
                n = s - 6
                if 0 <= n < 2 * NH:
                    lo, hi = COLS[0 if n < NH else 1]
                    a.wait_ge(o_out, n + 1)
                    if n:
                        a.wait_ge(osq_added, n)
                    nc.scalar.activation(sq[0][:, lo:hi], mixT[:, n % NH, lo:hi], ACT.Square).then_inc(osq_ready, 1)
                if s and s % 6 == 0:
                    csq(s // 3 - 2)
                    csq(s // 3 - 1)
                if s == 22:
                    root(ssum[0])
                    a.wait_ge(state_out, 32)
                    for k in range(AC):
                        a.wait_ge(normed, k + 1)
                        copy(ap[:, 0, k, :], mixT[:, k, :]).then_inc(mix_hi, 1)
            root(ssum[1])
            for k in range(CCH):
                a.wait_ge(normed, AC + k + 1)
                if k == 0:
                    a.wait_ge(mix_ready, AC)
                copy(cp[:, 0, k, :], mixT[:, AC + k, :]).then_inc(mix_hi, 1)
                if k == 1:
                    hi_part(U_QKV + U_CONV + 2)

            def sq2_chunk(c):
                a.wait_ge(x1_ready, c + 1)
                if c >= 2:
                    a.wait_ge(sq2_added, c - 1)
                nc.scalar.activation(sq2[c % 2], xT[:, c, :], ACT.Square).then_inc(sq2_ready, 1)

            for s in range(1, U_OUT + 1):
                if 1 < s < U_OUT - 1:
                    hi_part(U_QKV + U_CONV + s + 1)
                for chunk in DRAINED[s]:
                    sq2_chunk(chunk)
            root(rstd2)
            a.wait_ge(gains_ready, 2)
            for k in range(KC):
                if k % 3 < 2:
                    a.wait_ge(h2n_ready, k + 1)
                    for n, (lo, hi) in enumerate(COLS):
                        last = nc.scalar.activation(hT[:, k, lo:hi], hT[:, k, lo:hi], ACT.Identity,
                                                    scale=gain[:, 1, k, n:n + 1], bias=mod3[:, 3 * KC + k, n:n + 1])
                    last.then_inc(h2_act, 1)
            a.wait_ge(shifted, 1)
            nc.scalar.activation(lg, lg, ACT.Exp).then_inc(exp2_done, 1)
            rows_banks = [bank[5], bank[6], bank[7], bank[1]]
            for g in range(12):
                a.wait_ge(rows_turned, g + 1)
                kk = g % 4 * BLK
                copy(h2_rows[:, g // 4, kk:kk + BLK], rows_banks[g % 4][:, :]).then_inc(rows_out, 1)

            def xs_copy(i):
                for q in (0, 2):
                    a.wait_ge(gathered, 4 * i + (q + 1))
                    copy(xs[:, 4 * q:4 * q + 4, :], bank[4 + q][:, :].rearrange("p (k s) -> p k s", k=4)).then_inc(xs_act, 1)

            def silu(i, e, first):
                a.wait_ge(moe_used, PER_PAIR * i + (4 + 8 * e))
                if not (first and e == 0):
                    a.wait_ge(act_turned, 2 * i + e)
                nc.scalar.activation(act, bank[0][:, :], ACT.Silu).then_inc(sil_ready, 1)

            def rows_copy(i, e):
                a.wait_ge(moe_used, PER_PAIR * i + (16 + 8 * e))
                for half in range(2):
                    row = ES * (half ^ e)
                    last = copy(y_sb[half][row:row + ES, :].rearrange("p (b n) -> p b n", b=2), psum[row:row + ES, 2:4, :])
                last.then_inc(y_out, 1)

            def round_of(i, first=False, last_pair=False):
                silu(i, 0, first)
                for e in range(2):
                    a.wait_ge(give_turned, 2 * i + (e + 1))
                    copy(giveT[e], bank[2 + e][:, 0:T]).then_inc(giveT_ready, 1)
                silu(i, 1, first)
                rows_copy(i, 0)
                if not last_pair:
                    xs_copy(i + 1)
                    rows_copy(i, 1)

            def result_out(q):
                for t in range(NT):
                    a.wait_ge(last_turned, NT * q + t + 1)
                    copy(y_rows[:, t, q * BLK:(q + 1) * BLK], bank[4 + t][:, :]).then_inc(last_out, 1)

            xs_copy(0)
            round_of(0, first=True)
            with a.Fori(1, PAIRS - 1) as i:
                round_of(i)
            round_of(PAIRS - 1, last_pair=True)
            for q in range(4):
                a.wait_ge(moe_used, PER_PAIR * PAIRS - 3 + q)
                for half in range(2):
                    row = ES * (half ^ 1)
                    last = copy(y_sb[half][row:row + ES, q * UC:(q + 1) * UC], bank[LAST_BANKS[q]][row:row + ES, 0:UC])
                last.then_inc(y_last, 1)
                if q:
                    result_out(q - 1)
            result_out(3)

        @block.vector
        def _(v):
            ch = Chain(v, dve_chain)
            tt, ts, stt = nc.vector.tensor_tensor, nc.vector.tensor_scalar, nc.vector.scalar_tensor_tensor
            copy = nc.vector.tensor_copy

            v.wait_ge(vec_turned, 1)
            copy(vecT[:, :], bank[1][:, 0:V_ALL])
            copy(biasT[:, :], bank[2][:, 0:N_MOD * KC]).then_inc(vec_ready, 1)
            for g in range(0, 12, 2):
                v.wait_ge(x_turned, g + 1)
                t, kk = g // 4, g % 4 * 4
                copy(xT[:, kk:kk + 4, t * P:(t + 1) * P], bank[4 + g % 4][:, :].rearrange("p (j t) -> p j t", j=4))\
                    .then_inc(x_out_dve, 1)
            for k in range(KC):
                v.wait_ge(sq_ready, k + 1)
                if k == 0:
                    copy(ssum1, sq1[0]).then_inc(sq_added, 1)
                else:
                    v.wait_ge(sq_added, k)
                    tt(ssum1, ssum1, sq1[k % 2], ALU.add).then_inc(sq_added, 1)

            roots = [0]

            def invert_root(out, sums, n):
                roots[0] += 1
                ts(out, sums, 1.0 / n, EPS, ALU.mult, ALU.add).then_inc(var_ready, 1)
                v.wait_ge(std_ready, roots[0])
                ch.link(nc.vector.reciprocal(out, out))

            v.wait_ge(sums_done, 1)
            invert_root(ssum1, bank[3][:, 0:T], D)
            v.wait_ge(x_out_act, 6)
            for k in range(KC):
                last = tt(xhatT[:, k, :], xT[:, k, :], ssum1, ALU.mult)
            ch.link(last)

            def lo_part(u):
                v.wait_ge(hi_ready, u + 1)
                tt(w_part(u, 1), raw_unit(u), w_part(u, 0).bitcast(F32), ALU.subtract).then_inc(lo_ready, 1)

            def mod_out(m):
                v.wait_ge(mod_turned, m + 1)
                src = bank[(2, 3, 0, 0, 0, 2)[m]][:, :].rearrange("p (c j n) -> p j c n", c=4, j=4)
                four = [P, 4, 4, 2]
                ins = tt(mod3[:, m * KC:(m + 1) * KC, :].rearrange("p (j c) n -> p j c n", j=4), src[:, :, :, 0:2],
                         biasT[:, m * KC:(m + 1) * KC].rearrange("p (j c) -> p j c", j=4).unsqueeze(3).to_broadcast(four), ALU.add)
                ins.then_inc(mod_read, 1)
                v.wait_ge(mod_read, m + 1)

            def gains(which, scale_m, row):
                stt(gain[:, which, :, :], mod3[:, scale_m * KC:(scale_m + 1) * KC, :], 1.0,
                    vecT[:, row:row + KC].unsqueeze(2).to_broadcast([P, KC, 2]), ALU.add, ALU.mult).then_inc(gains_ready, 1)
                v.wait_ge(gains_ready, which + 1)

            v.wait_ge(w_used, N_ADA1)
            for m in range(2):
                copy(mod_rows[m], bank[m][:, :]).then_inc(mod_rows_out, 1)
            lo_part(0)
            for m in range(2):
                mod_out(m)
            gains(0, 1, V_G1)
            def h_even(k):
                for n, (lo, hi) in enumerate(COLS):
                    last = ts(xhatT[:, k, lo:hi], xhatT[:, k, lo:hi], gain[:, 0, k, n:n + 1], mod3[:, k, n:n + 1], ALU.mult, ALU.add)
                last.then_inc(h_dve, 1)

            h_even(0)
            for k in range(0, KC, 2):
                if k + 2 < KC:
                    h_even(k + 2)
                for kk in (k, k + 1):
                    v.wait_ge(h_hi, kk + 1)
                    tt(hp[:, 1, kk, :], xhatT[:, kk, :], hp[:, 0, kk, :].bitcast(F32), ALU.subtract).then_inc(h_parts_ready, 1)
                if k == 6:
                    lo_part(1)

            def prep(b):
                src, g0 = (q_rows[:, :, b * UC:(b + 1) * UC], 0) if b < 4 else (kv_rows[:, :, 0:D_KV], HD)
                rows = src.rearrange("p t (h d) -> p t h d", d=HD)
                shape = [P, NT, 2, HD]
                if b == 0:
                    v.wait_ge(cache_in, 64)
                v.wait_ge(qkv_out, NT * (b + 1))
                squares = tmp[:, 0:NT * UC].rearrange("p (t h d) -> p t h d", t=NT, d=HD)
                sums = stat[:, 0:2 * NT]
                ch.link(tt(squares, rows, rows, ALU.mult))
                ch.link(nc.vector.tensor_reduce(sums.rearrange("p (t h) -> p t h", t=NT), squares, AX_X, ALU.add))
                invert_root(sums, sums, HD)
                ch.link(tt(rows, rows, sums.rearrange("p (t h) -> p t h", t=NT).unsqueeze(3).to_broadcast(shape), ALU.mult))
                ch.link(tt(rows, rows, gqk[:, g0:g0 + HD].unsqueeze(1).unsqueeze(1).to_broadcast(shape), ALU.mult))
                table = rope.rearrange("p (t x) -> p t x", t=NT - 1)
                four = [P, NT - 1, 2, 32]
                for axis in range(2):
                    x1, x2 = (rows[:, 1:NT, :, 64 * axis + 32 * n:64 * axis + 32 * n + 32] for n in range(2))
                    cos, sin = (table[:, :, o + axis * 32:o + axis * 32 + 32].unsqueeze(2).to_broadcast(four) for o in (0, 64))
                    ta = [tmp[:, n * P:(n + 1) * P].rearrange("p (t h d) -> p t h d", t=NT - 1, d=32) for n in range(4)]
                    tt(ta[0], x1, cos, ALU.mult)
                    tt(ta[1], x2, sin, ALU.mult)
                    tt(ta[2], x1, sin, ALU.mult)
                    ch.link(tt(ta[3], x2, cos, ALU.mult))
                    tt(x1, ta[0], ta[1], ALU.subtract)
                    last = tt(x2, ta[2], ta[3], ALU.add)
                    if axis == 0:
                        ch.link(last)
                last.then_inc(qk_ready, 1)
                v.wait_ge(qk_ready, b + 1)

            def after_events(lo, hi):
                for n in range(lo, min(hi, EVENTS_FRONT)):
                    m, k = 2 + n // (KC + 1), n % (KC + 1)
                    if k == KC - 1:
                        v.wait_ge(ada_free, 2 + KC * (m - 1))
                        copy(mod_rows[0], bank[0][:, :]).then_inc(mod_rows_out, 1)
                    if k == KC:
                        mod_out(m)

            for u in range(U_QKV):
                if u:
                    lo_part(u + 1)
                after_events(2 * u, 2 * u + 2)
                if u and u % 2 == 0:
                    prep(u // 2 - 1)

            def taps(m):
                j = m % 2
                tap = [vecT[:, V_TAP + w * CCH + m:V_TAP + w * CCH + m + 1] for w in range(3)]
                v.wait_ge(conv_out, m // 2 * 6 + m % 2 + 4)
                ch.link(ts(cv, cu[:, j, :], tap[1], None, ALU.mult))
                for lo, hi in COLS:
                    last = stt(cv[:, lo + 1:hi], cu[:, j, lo:hi - 1], tap[0], cv[:, lo + 1:hi], ALU.mult, ALU.add)
                ch.link(last)
                for lo, hi in COLS:
                    last = stt(cv[:, lo:hi - 1], cu[:, j, lo + 1:hi], tap[2], cv[:, lo:hi - 1], ALU.mult, ALU.add)
                ch.link(last)

            def conv_chunk(b, j):
                src = bank[1 + j][:, 0:T]
                if j == 0:
                    v.wait_ge(conv_acc, b + 1)
                else:
                    v.wait_ge(unit_used, U_QKV + 2 * b + 2)
                if b % 3 == 0:
                    copy(cu[:, j, :], src).then_inc(conv_out, 1)
                elif b % 3 == 1:
                    v.wait_ge(conv_out, 2 * b + j - 1)
                    tt(cu[:, j, :], src, cu[:, j, :], ALU.mult).then_inc(conv_out, 1)
                else:
                    m = b // 3 * 2 + j
                    tt(mixT[:, AC + m, :], src, cv, ALU.mult).then_inc(conv_out, 1)
                    if j == 0:
                        taps(m + 1)

            def csq_add(m):
                v.wait_ge(csq_ready, m + 1)
                if m == 0:
                    copy(ssum[1], sq[1]).then_inc(csq_added, 1)
                else:
                    v.wait_ge(csq_added, m)
                    tt(ssum[1], ssum[1], sq[1], ALU.add).then_inc(csq_added, 1)

            def mix_lo(k):
                v.wait_ge(mix_hi, k + 1)
                parts, n = (ap, k) if k < AC else (cp, k - AC)
                tt(parts[:, 1, n, :], mixT[:, k, :], parts[:, 0, n, :].bitcast(F32), ALU.subtract).then_inc(mix_ready, 1)

            for s in range(U_CONV + 1):
                if s and s % 2 == 0:
                    conv_chunk(s // 2 - 1, 1)
                if s == U_CONV:
                    v.wait_ge(conv_out, 24)
                    for k in range(LO_EARLY, AC):
                        mix_lo(k)
                n = s - 4
                if 0 <= n < 2 * NH:
                    tiles, nk = (1, 1) if n < NH else (2, 3)
                    v.wait_ge(score_done, n + 1)
                    for i in range(tiles):
                        last = nc.vector.tensor_reduce(stat[:, 10 + i:11 + i], bank[3 + i][:, 0:nk * P], AX_X, ALU.max)
                    ch.link(last)
                    ts(stat[:, 12:12 + tiles], stat[:, 10:10 + tiles], -SCALE, None, ALU.mult).then_inc(max_ready, 1)
                if s < U_CONV:
                    lo_part(U_QKV + s + 1)
                    after_events(2 * (U_QKV + s), 2 * (U_QKV + s) + 2)
                if 0 <= n < 2 * NH:
                    v.wait_ge(exp_done, n + 1)
                    ch.link(nc.vector.reciprocal(stat[:, 16:16 + tiles], stat[:, 14:14 + tiles]))
                    for i in range(tiles):
                        last = ts(prob[:, i, 0:nk * P], prob[:, i, 0:nk * P], stat[:, 16 + i:17 + i], None, ALU.mult)
                    last.then_inc(prob_ready, 1)
                n = s - 6
                if 0 <= n < 2 * NH:
                    lo, hi = COLS[0 if n < NH else 1]
                    v.wait_ge(o_done, n + 1)
                    copy(mixT[:, n % NH, lo:hi], bank[7][:, 0:hi - lo]).then_inc(o_out, 1)
                    v.wait_ge(osq_ready, n + 1)
                    if n % NH == 0:
                        copy(ssum[0][:, lo:hi], sq[0][:, lo:hi]).then_inc(osq_added, 1)
                    else:
                        v.wait_ge(osq_added, n)
                        tt(ssum[0][:, lo:hi], ssum[0][:, lo:hi], sq[0][:, lo:hi], ALU.add).then_inc(osq_added, 1)
                if s and s % 6 == 0:
                    csq_add(s // 3 - 2)
                    csq_add(s // 3 - 1)
                if s == 22:
                    v.wait_ge(sums_done, 2)
                    invert_root(ssum[0], bank[3][:, 0:T], D_ATTN)
                    for k in range(AC):
                        stt(mixT[:, k, :], mixT[:, k, :], vecT[:, V_GA + k:V_GA + k + 1], ssum[0], ALU.mult, ALU.mult)\
                            .then_inc(normed, 1)
                if s % 6 == 4:
                    taps(s // 6 * 2)
                if s % 2:
                    conv_chunk(s // 2, 0)
                if s == U_CONV - 1:
                    for k in range(LO_EARLY):
                        mix_lo(k)
            lo_part(U_QKV + U_CONV + 1)
            v.wait_ge(sums_done, 3)
            invert_root(ssum[1], bank[4][:, 0:T], D_CONV)
            for k in range(CCH):
                stt(mixT[:, AC + k, :], mixT[:, AC + k, :], vecT[:, V_GC + k:V_GC + k + 1], ssum[1], ALU.mult, ALU.mult)\
                    .then_inc(normed, 1)
                if k:
                    mix_lo(AC + k - 1)
                if k == 2:
                    lo_part(U_QKV + U_CONV + 2)
            mix_lo(KC - 1)

            ch.link(nc.vector.memset(ssum2, 0.0))

            def x1_chunk(c):
                if c % 2 == 0:
                    v.wait_ge(out_acc, c // 2 + 1)
                else:
                    v.wait_ge(unit_used, U_QKV + U_CONV + (3 + c // 2 if c < 4 else c + 1))
                src = bank[FIRST_BANKS[c] if c < 4 else 1 + c % 2]
                for n, (lo, hi) in enumerate(COLS):
                    last = stt(xT[:, c, lo:hi], src[:, lo:hi], mod3[:, 2 * KC + c, n:n + 1], xT[:, c, lo:hi],
                               ALU.mult, ALU.add)
                last.then_inc(x1_ready, 1)

            def sq2_add(c):
                v.wait_ge(sq2_ready, c + 1)
                if c:
                    v.wait_ge(sq2_added, c)
                tt(ssum2, ssum2, sq2[c % 2], ALU.add).then_inc(sq2_added, 1)

            for s in range(1, U_OUT + 1):
                for c in DRAINED[s]:
                    if c % 2:
                        x1_chunk(c)
                if 1 < s < U_OUT - 1:
                    lo_part(U_QKV + U_CONV + s + 1)
                for c in DRAINED[s]:
                    if c % 2 == 0:
                        x1_chunk(c)
                for c in DRAINED[s - 1]:
                    if c < KC - 2:
                        sq2_add(c)

            gains(1, 4, V_G2)
            v.wait_ge(sums_done, 4)
            v.wait_ge(unit_used, U_ALL)
            invert_root(rstd2, bank[3][:, 0:T], D)
            v.wait_ge(x1_ready, KC)
            for k in range(KC):
                tt(hT[:, k, :], xT[:, k, :], rstd2, ALU.mult).then_inc(h2n_ready, 1)
                if k % 3 == 0 and k:
                    kk = k - 1
                    v.wait_ge(h2n_ready, k)
                    for n, (lo, hi) in enumerate(COLS):
                        last = ts(hT[:, kk, lo:hi], hT[:, kk, lo:hi], gain[:, 1, kk, n:n + 1], mod3[:, 3 * KC + kk, n:n + 1],
                                  ALU.mult, ALU.add)
                    last.then_inc(h2_dve, 1)

            v.wait_ge(logits_done, 1)
            copy(lg_parts, bank[4][:, 0:T]).then_inc(logits_out, 1)
            v.wait_ge(logits_turned, 1)
            parts = bank[3][:, 0:T].rearrange("p (t j e) -> p t e j", t=NT, j=4)
            ch.link(nc.vector.tensor_reduce(lg, parts[:, :, 0:NE, :], AX_X, ALU.add))
            ch.link(nc.vector.tensor_reduce(r_small[:, 0:3], lg, AX_X, ALU.max))
            tt(lg, lg, r_small[:, 0:3].unsqueeze(2).to_broadcast([P, NT, NE]), ALU.subtract).then_inc(shifted, 1)
            v.wait_ge(exp2_done, 1)
            ch.link(nc.vector.tensor_reduce(r_small[:, 3:6], lg, AX_X, ALU.add))
            ch.link(nc.vector.reciprocal(r_small[:, 6:9], r_small[:, 3:6]))
            tt(lg, lg, r_small[:, 6:9].unsqueeze(2).to_broadcast([P, NT, NE]), ALU.mult).then_inc(aff_ready, 1)
            v.wait_ge(aff_ready, 1)

            def by_pair(ap):
                return ap[:, 0:6 * PAIRS].rearrange("p (i t e) -> p t i e", t=NT, e=2)
            ch.link(copy(by_pair(affP), lg.rearrange("p t (i e) -> p t i e", e=2)))

            v.wait_ge(aff_turned, 1)
            copy(affT, bank[3][0:NE, 0:T])
            ch.link(copy(work, bank[3][0:NE, 0:T]))
            for cap, (lo, hi) in ((CAP_CTX, COLS[0]), (CAP_LAT, COLS[1])):
                for _ in range(cap // 8):
                    ch.link(nc.vector.max(top8, work[:, lo:hi]))
                    ch.link(nc.vector.match_replace(work[:, lo:hi], top8, work[:, lo:hi], -1.0))
            ch.link(ts(mask, work, 0.0, None, ALU.is_lt))
            for first, (lo, hi) in ((0.0, COLS[0]), (float(CAP_CTX), COLS[1])):
                last = nc.vector.tensor_tensor_scan(rank[:, lo:hi], mask[:, lo:hi], affT[:, lo:hi], first, ALU.add, ALU.bypass)
            ch.link(last)
            ch.link(tt(rank, rank, mask, ALU.mult))
            ts(rank, rank, -1.0, None, ALU.add).then_inc(rank_ready, 1)
            v.wait_ge(rank_turned, 1)
            copy(by_pair(slotP), bank[4][:, 0:NT * NE].rearrange("p (t i e) -> p t i e", t=NT, e=2)).then_inc(routed, 1)

            def make(i):
                six = [P, 6, ES]
                pick3 = pick.rearrange("p (a s) -> p a s", a=6)
                tt(pick3, slotP[:, bass.ds(6 * i, 6)].unsqueeze(2).to_broadcast(six),
                   iota[:, :].unsqueeze(1).to_broadcast(six), ALU.is_equal).then_inc(pick_ready, 1)
                v.wait_ge(pick_ready, i + 1)
                aff = affP[:, bass.ds(6 * i, 6)].rearrange("p (t e) -> p t e", e=2)
                by_tile = pick.rearrange("p (t e s) -> p t e s", t=NT, e=2)
                tt(give[:, :, 0:2 * ES].rearrange("p t (e s) -> p t e s", e=2), by_tile,
                   aff.unsqueeze(3).to_broadcast([P, NT, 2, ES]), ALU.mult)
                last = tt(give[:, :, 2 * ES:], by_tile[:, :, 0, :], aff[:, :, 0:1].to_broadcast([P, NT, ES]), ALU.mult)
                last.then_inc(give_ready, 1)

            def xs_copy(i):
                for q in (1, 3):
                    v.wait_ge(gathered, 4 * i + (q + 1))
                    copy(xs[:, 4 * q:4 * q + 4, :], bank[4 + q][:, :].rearrange("p (k s) -> p k s", k=4)).then_inc(xs_dve, 1)

            def add(k, b):
                for n, (lo, hi) in enumerate(COLS):
                    last = stt(xT[:, k, lo:hi], bank[b][:, lo:hi], mod3[:, 5 * KC + k, n:n + 1], xT[:, k, lo:hi],
                               ALU.mult, ALU.add)
                last.then_inc(added, 1)

            def round_of(i, first=False, last_pair=False):
                for e in range(2):
                    v.wait_ge(sil_ready, 2 * i + (e + 1))
                    v.wait_ge(moe_used, PER_PAIR * i + (8 if e == 0 else 20))
                    tt(act, bank[1][:, :], act, ALU.mult).then_inc(act_ready, 1)
                    if e == 0:
                        if not first:
                            for k in range(KC):
                                v.wait_ge(sent, 16 * i + (k - 15))
                                add(k, 4 + k % 4)
                        if not last_pair:
                            v.wait_ge(give_turned, 2 * i + 2)
                            make(i + 1)
                    elif not last_pair:
                        xs_copy(i + 1)
                    v.wait_ge(act_turned, 2 * i + (e + 1))
                    copy(actT, bank[4][:, :]).then_inc(actT_ready, 1)

            v.wait_ge(routed, 1)
            v.wait_ge(rows_out, 12)
            v.wait_ge(ada_free, 2 + 64)
            make(0)
            copy(act, bank[0][:, :]).then_inc(mod_rows_out, 1)
            xs_copy(0)
            mod_out(N_MOD - 1)
            round_of(0, first=True)
            with v.Fori(1, PAIRS - 1) as i:
                round_of(i)
            round_of(PAIRS - 1, last_pair=True)
            for q in range(4):
                for n, (k, b) in enumerate(zip(chunks_of(q), [4, 5, 6, 7] if q == 0 else [7, 4, 5, 6])):
                    v.wait_ge(sent, 16 * (PAIRS - 1) + 4 * q + n + 1)
                    add(k, b)


def constants():
    out = np.zeros((P, C_ALL), np.float32)
    out[:, C_ID:C_ID + P] = np.eye(P, dtype=np.float32)
    half = HD // 2
    inv = (np.float32(10000.0) ** (-np.arange(0, half, 2, dtype=np.float32) / np.float32(half))).astype(np.float32)
    pos = np.arange(T_LAT)
    ang = np.concatenate([(pos // GRID_W).astype(np.float32)[:, None] * inv,
                          (pos % GRID_W).astype(np.float32)[:, None] * inv], axis=1)
    for n in range(T_LAT // P):
        rows = ang[n * P:(n + 1) * P]
        o = C_ROPE + n * P
        out[:, o:o + 64] = np.cos(rows)
        out[:, o + 64:o + 128] = np.sin(rows)
    out[:, C_IOTA:] = np.arange(ES, dtype=np.float32)
    return out


_INS = ["x_prompt", "x_sample", "cache_k", "cache_v", "c", "c_ctx", "w_ada", "b_ada", "g_norm1", "w_in", "g_q", "g_k",
        "conv_w", "g_attn_out", "g_conv_out", "w_out", "g_norm2", "w_router", "w_gate", "w_up", "w_down"]
_OUTS = [(1, T_CTX, D), (1, T_LAT, D), (1, 1, T_CTX, NKV, HD), (1, 1, T_CTX, NKV, HD)]


def kernel(**inputs):
    import concourse.bacc as bacc
    from concourse.bass_utils import run_bass_kernel_spmd

    nc = bacc.Bacc("TRN2", target_bir_lowering=False, num_devices=1)
    arrays, args = {}, []
    for name in _INS + ["consts"]:
        a = constants() if name == "consts" else np.ascontiguousarray(inputs[name])
        arrays[f"in_{name}"] = a
        args.append(nc.dram_tensor(f"in_{name}", a.shape, mybir.dt.from_np(a.dtype), kind="ExternalInput").ap())
    for i, shape in enumerate(_OUTS):
        args.append(nc.dram_tensor(f"out_{i}", shape, F32, kind="ExternalOutput").ap())
    build(nc, *args)
    r = run_bass_kernel_spmd(nc, [arrays], core_ids=[0])
    return tuple(r.results[0][f"out_{i}"] for i in range(len(_OUTS)))
```
